# Optimizing a Trainium2 kernel written in Bass

```python
import math
import jax, jax.numpy as jnp
from jax import lax
import numpy as np

D_MODEL = 1024
BATCH = 1
SEQ = 256
DEPTH = 2

N_MIXERS = 2
SSM_EXPAND = 2
D_INNER = SSM_EXPAND * D_MODEL
HEAD_DIM = 64
N_SSM_HEADS = D_INNER // HEAD_DIM
N_GROUPS = 4
HEADS_PER_GROUP = N_SSM_HEADS // N_GROUPS
D_STATE = 128
SSM_CONV = 4
CONV_DIM = D_INNER + 2 * N_GROUPS * D_STATE
IN_PROJ_DIM = 2 * D_INNER + 2 * N_GROUPS * D_STATE + N_SSM_HEADS
CHUNK = 128
CF_KERNEL = 31
N_MEM = 256
XA_HEADS = 4
XA_HEAD_DIM = D_MODEL // XA_HEADS
D_FF = 2816
FFN_CONV = 3
EPS = 1e-6


def rmsnorm(x, g):
    xf = x.astype(jnp.float32)
    y = xf * lax.rsqrt(jnp.mean(xf * xf, axis=-1, keepdims=True) + EPS)
    return (y * g.astype(jnp.float32)).astype(x.dtype)

def layernorm(x, g, b):
    xf = x.astype(jnp.float32)
    mu = jnp.mean(xf, axis=-1, keepdims=True)
    var = jnp.mean(jnp.square(xf - mu), axis=-1, keepdims=True)
    y = (xf - mu) * lax.rsqrt(var + EPS)
    return (y * g.astype(jnp.float32) + b.astype(jnp.float32)).astype(x.dtype)

def causal_dwconv(x, w, b):
    K, C = w.shape
    y = lax.conv_general_dilated(
        x, w[:, None, :].astype(x.dtype), window_strides=(1,), padding=[(K - 1, 0)],
        dimension_numbers=("NWC", "WIO", "NWC"), feature_group_count=C)
    return y + b.astype(x.dtype)

def ssd_mixer(h, in_w, conv_w, conv_b, dt_bias, A_log, D_skip, norm_g, out_w):
    Bsz, L, _ = h.shape
    nc = L // CHUNK
    G, Hg, P, N, Q = N_GROUPS, HEADS_PER_GROUP, HEAD_DIM, D_STATE, CHUNK
    f32 = jnp.float32
    proj = h @ in_w
    z, xBC, dt_raw = jnp.split(proj, [D_INNER, D_INNER + CONV_DIM], axis=-1)
    xBC = jax.nn.silu(causal_dwconv(xBC, conv_w, conv_b))
    xs, Bm, Cm = jnp.split(xBC, [D_INNER, D_INNER + G * N], axis=-1)
    xs = xs.astype(f32).reshape(Bsz, nc, Q, G, Hg, P)
    Bm = Bm.astype(f32).reshape(Bsz, nc, Q, G, N)
    Cm = Cm.astype(f32).reshape(Bsz, nc, Q, G, N)
    dt = jax.nn.softplus(dt_raw.astype(f32) + dt_bias.astype(f32)).reshape(Bsz, nc, Q, G, Hg)
    A = -jnp.exp(A_log.astype(f32)).reshape(G, Hg)
    cs = jnp.cumsum(dt * A, axis=2)
    xdt = xs * dt[..., None]
    tri = jnp.tril(jnp.ones((Q, Q), dtype=bool))
    seg = cs[:, :, :, None] - cs[:, :, None, :]
    decay = jnp.exp(jnp.where(tri[None, None, :, :, None, None], seg, -jnp.inf))
    CB = jnp.einsum("bcign,bcjgn->bcijg", Cm, Bm)
    y_diag = jnp.einsum("bcijgh,bcjghp->bcighp", CB[..., None] * decay, xdt)
    decay_to_end = jnp.exp(cs[:, :, -1:] - cs)
    states = jnp.einsum("bcjgn,bcjgh,bcjghp->bcghpn", Bm, decay_to_end, xdt)
    chunk_decay = jnp.exp(cs[:, :, -1])

    def step(carry, inp):
        st, dec = inp
        return carry * dec[..., None, None] + st, carry

    h0 = jnp.zeros((Bsz, G, Hg, P, N), f32)
    _, prev = lax.scan(step, h0, (jnp.swapaxes(states, 0, 1), jnp.swapaxes(chunk_decay, 0, 1)))
    prev = jnp.swapaxes(prev, 0, 1)
    y_off = jnp.einsum("bcign,bcghpn,bcigh->bcighp", Cm, prev, jnp.exp(cs))
    y = y_diag + y_off + xs * D_skip.astype(f32).reshape(G, Hg)[:, :, None]
    y = y.reshape(Bsz, L, D_INNER).astype(h.dtype)
    y = rmsnorm(y * jax.nn.silu(z), norm_g)
    return y @ out_w

def conformer_conv(h, pw1_w, pw1_b, dw_w, dw_b, ln_g, ln_b, pw2_w, pw2_b):
    u = h @ pw1_w + pw1_b
    a, gt = jnp.split(u, 2, axis=-1)
    c = causal_dwconv(a * jax.nn.sigmoid(gt), dw_w, dw_b)
    c = jax.nn.silu(layernorm(c, ln_g, ln_b))
    return c @ pw2_w + pw2_b

def mem_xattn(h, mem, mem_g, q_w, kv_w, o_w):
    Bsz, L, _ = h.shape
    m = rmsnorm(mem, mem_g)
    q = (h @ q_w).reshape(Bsz, L, XA_HEADS, XA_HEAD_DIM)
    k, v = jnp.split(m @ kv_w, 2, axis=-1)
    k = k.reshape(Bsz, N_MEM, XA_HEADS, XA_HEAD_DIM)
    v = v.reshape(Bsz, N_MEM, XA_HEADS, XA_HEAD_DIM)
    s = jnp.einsum("blhd,bmhd->bhlm", q, k).astype(jnp.float32) * (XA_HEAD_DIM ** -0.5)
    p = jax.nn.softmax(s, axis=-1).astype(v.dtype)
    o = jnp.einsum("bhlm,bmhd->blhd", p, v).reshape(Bsz, L, D_MODEL)
    return o @ o_w

def conv_ffn(h, in_w, conv_w, conv_b, out_w):
    u = causal_dwconv(h @ in_w, conv_w, conv_b)
    g, v = jnp.split(u, 2, axis=-1)
    return (jax.nn.silu(g) * v) @ out_w

def first_inputs(seed: int = 0) -> dict:
    key = jax.random.key(seed)
    ks = jax.random.split(key, 32)
    nA = (DEPTH + 1) // 2
    nB = DEPTH // 2
    D = D_MODEL

    def w(k, shape, fan_in):
        return jax.random.normal(k, shape, jnp.float32) * (fan_in ** -0.5)

    def gain(k, shape):
        return 1.0 + 0.02 * jax.random.normal(k, shape, jnp.float32)

    def bias(k, shape):
        return 0.02 * jax.random.normal(k, shape, jnp.float32)

    log_dt = jax.random.uniform(ks[5], (nA, N_SSM_HEADS), jnp.float32, math.log(1e-3), math.log(1e-1))
    dt0 = jnp.exp(log_dt)
    return {
        "x": jax.random.normal(ks[0], (BATCH, SEQ, D), jnp.float32),
        "mem": jax.random.normal(ks[1], (BATCH, N_MEM, D), jnp.float32),
        "norm_g": gain(ks[2], (DEPTH, 6, D)),
        "ssm_in_w": w(ks[3], (nA, D, IN_PROJ_DIM), D),
        "ssm_conv_w": w(ks[4], (nA, SSM_CONV, CONV_DIM), SSM_CONV),
        "ssm_conv_b": bias(ks[6], (nA, CONV_DIM)),
        "ssm_dt_bias": dt0 + jnp.log(-jnp.expm1(-dt0)),
        "ssm_A_log": jnp.log(jax.random.uniform(ks[7], (nA, N_SSM_HEADS), jnp.float32, 1.0, 16.0)),
        "ssm_D": 1.0 + 0.1 * jax.random.normal(ks[8], (nA, N_SSM_HEADS), jnp.float32),
        "ssm_norm_g": gain(ks[9], (nA, D_INNER)),
        "ssm_out_w": w(ks[10], (nA, D_INNER, D), D_INNER),
        "cf_pw1_w": w(ks[11], (nB, D, 2 * D), D),
        "cf_pw1_b": bias(ks[12], (nB, 2 * D)),
        "cf_dw_w": w(ks[13], (nB, CF_KERNEL, D), CF_KERNEL),
        "cf_dw_b": bias(ks[14], (nB, D)),
        "cf_ln_g": gain(ks[15], (nB, D)),
        "cf_ln_b": bias(ks[16], (nB, D)),
        "cf_pw2_w": w(ks[17], (nB, D, D), D),
        "cf_pw2_b": bias(ks[18], (nB, D)),
        "xa_mem_g": gain(ks[19], (DEPTH, D)),
        "xa_q_w": w(ks[20], (DEPTH, D, D), D),
        "xa_kv_w": w(ks[21], (DEPTH, D, 2 * D), D),
        "xa_o_w": w(ks[22], (DEPTH, D, D), D),
        "ffn_in_w": w(ks[23], (DEPTH, D, 2 * D_FF), D),
        "ffn_conv_w": w(ks[24], (DEPTH, FFN_CONV, 2 * D_FF), FFN_CONV),
        "ffn_conv_b": bias(ks[25], (DEPTH, 2 * D_FF)),
        "ffn_out_w": w(ks[26], (DEPTH, D_FF, D), D_FF),
    }

def first_block(x, mem, norm_g,
              ssm_in_w, ssm_conv_w, ssm_conv_b, ssm_dt_bias, ssm_A_log, ssm_D, ssm_norm_g, ssm_out_w,
              cf_pw1_w, cf_pw1_b, cf_dw_w, cf_dw_b, cf_ln_g, cf_ln_b, cf_pw2_w, cf_pw2_b,
              xa_mem_g, xa_q_w, xa_kv_w, xa_o_w,
              ffn_in_w, ffn_conv_w, ffn_conv_b, ffn_out_w):
    for i in range(DEPTH):
        g = norm_g[i]
        j = i // N_MIXERS
        h = rmsnorm(x, g[0])
        if i % N_MIXERS == 0:
            mix = ssd_mixer(h, ssm_in_w[j], ssm_conv_w[j], ssm_conv_b[j], ssm_dt_bias[j],
                            ssm_A_log[j], ssm_D[j], ssm_norm_g[j], ssm_out_w[j])
        else:
            mix = conformer_conv(h, cf_pw1_w[j], cf_pw1_b[j], cf_dw_w[j], cf_dw_b[j],
                                 cf_ln_g[j], cf_ln_b[j], cf_pw2_w[j], cf_pw2_b[j])
        x = x + rmsnorm(mix, g[1])
        a = mem_xattn(rmsnorm(x, g[2]), mem, xa_mem_g[i], xa_q_w[i], xa_kv_w[i], xa_o_w[i])
        x = x + rmsnorm(a, g[3])
        f = conv_ffn(rmsnorm(x, g[4]), ffn_in_w[i], ffn_conv_w[i], ffn_conv_b[i], ffn_out_w[i])
        x = x + rmsnorm(f, g[5])
    return x


_first_inputs = first_inputs


def first_inputs(seed=0):
    import zlib

    import numpy as np

    out = dict(_first_inputs(seed))
    spreads = {}
    factors = {'ssm_norm_g': 3.286,
     'cf_pw1_b': 5.083,
     'cf_dw_b': 2.837,
     'cf_ln_g': 5.01,
     'cf_ln_b': 6.078,
     'cf_pw2_b': 3.676,
     'ffn_conv_b': 2.96}
    for name, (base, spread) in spreads.items():
        noise = np.random.default_rng([zlib.crc32(name.encode()), seed]).standard_normal(out[name].shape)
        drawn = base * np.exp(spread * noise) if base else spread * noise
        out[name] = __import__('jax').numpy.asarray(drawn.astype(out[name].dtype))
    for name, factor in factors.items():
        out[name] = (out[name] * factor).astype(out[name].dtype)
    return out


_narrow_inputs = first_inputs


def first_inputs(seed=0):

    out = dict(_narrow_inputs(seed))
    wider = {'ssm_norm_g': 3.72, 'cf_ln_g': 6.62, 'cf_ln_b': 5.59, 'cf_pw2_b': 6.59}
    for name, times in wider.items():
        mean = out[name].mean()
        out[name] = (mean + times * (out[name] - mean)).astype(out[name].dtype)
    return out


PLE_DIM = 256
D_FF_2 = 4 * D_MODEL
NORM_EPS = 1e-6
ROPE_THETA = 500000.0
ROPE_FRACTION = 4
Q_BLOCK = 128

SB_HEADS = 8
SB_HEAD_DIM = 64
DIFF_HEADS = 4
DIFF_HEAD_DIM = 64
DIFF_V_DIM = 2 * DIFF_HEAD_DIM
SB_WIDTH = SB_HEADS * SB_HEAD_DIM
DIFF_QK_WIDTH = DIFF_HEADS * 2 * DIFF_HEAD_DIM
DIFF_V_WIDTH = DIFF_HEADS * DIFF_V_DIM
EVEN_IN_WIDTH = 3 * SB_WIDTH + 2 * DIFF_QK_WIDTH + DIFF_V_WIDTH
EVEN_OUT_WIDTH = SB_WIDTH + DIFF_V_WIDTH

MOBA_HEADS = 16
MOBA_HEAD_DIM = 64
MOBA_WIDTH = MOBA_HEADS * MOBA_HEAD_DIM
MOBA_BLOCK = 256
MOBA_TOPK = 3
MOBA_Q_CHUNK = 64

N_EVEN = (DEPTH + 1) // 2
N_ODD = DEPTH // 2


def rms_norm(x, g):
    xf = x.astype(jnp.float32)
    y = xf * lax.rsqrt(jnp.mean(xf * xf, axis=-1, keepdims=True) + NORM_EPS)
    return (y * g.astype(jnp.float32)).astype(x.dtype)

def rope_tables(positions, head_dim):
    rot = head_dim // ROPE_FRACTION
    inv_freq = ROPE_THETA ** (-(jnp.arange(0, rot, 2, dtype=jnp.float32) / rot))
    ang = positions.astype(jnp.float32)[..., None] * inv_freq
    return jnp.cos(ang), jnp.sin(ang)

def apply_partial_rope(x, cos, sin):
    half = cos.shape[-1]
    rot = 2 * half
    c = cos[:, :, None, :]
    s = sin[:, :, None, :]
    x1 = x[..., :half].astype(jnp.float32)
    x2 = x[..., half:rot].astype(jnp.float32)
    r = jnp.concatenate([x1 * c - x2 * s, x1 * s + x2 * c], axis=-1).astype(x.dtype)
    return jnp.concatenate([r, x[..., rot:]], axis=-1)

def to_heads(t, n_heads):
    b, s, _ = t.shape
    return t.reshape(b, s, n_heads, -1).transpose(0, 2, 1, 3)

def from_heads(t):
    b, h, s, d = t.shape
    return t.transpose(0, 2, 1, 3).reshape(b, s, h * d)

def stick_breaking_attention(q, k, v):
    B, H, S, d = q.shape
    nqb = S // Q_BLOCK
    scale = d ** -0.5
    kpos = jnp.arange(S)
    qb = q.reshape(B, H, nqb, Q_BLOCK, d).transpose(2, 0, 1, 3, 4)

    def one_block(args):
        qi, bi = args
        qpos = bi * Q_BLOCK + jnp.arange(Q_BLOCK)
        z = jnp.einsum('bhqd,bhkd->bhqk', qi, k).astype(jnp.float32) * scale
        past = kpos[None, :] < qpos[:, None]
        log_keep = jnp.where(past, jax.nn.log_sigmoid(-z), 0.0)
        tail = lax.cumsum(log_keep, axis=3, reverse=True) - log_keep
        w = jnp.where(past, jnp.exp(jax.nn.log_sigmoid(z) + tail), 0.0)
        return jnp.einsum('bhqk,bhkd->bhqd', w.astype(v.dtype), v)

    out = lax.map(one_block, (qb, jnp.arange(nqb)))
    return out.transpose(1, 2, 0, 3, 4).reshape(B, H, S, d)

def diff_attention(q1, q2, k1, k2, v, lam):
    B, H, S, d = q1.shape
    nqb = S // Q_BLOCK
    scale = d ** -0.5
    kpos = jnp.arange(S)
    q1b = q1.reshape(B, H, nqb, Q_BLOCK, d).transpose(2, 0, 1, 3, 4)
    q2b = q2.reshape(B, H, nqb, Q_BLOCK, d).transpose(2, 0, 1, 3, 4)
    lam_b = lam[None, :, None, None]

    def one_block(args):
        q1i, q2i, bi = args
        qpos = bi * Q_BLOCK + jnp.arange(Q_BLOCK)
        causal = kpos[None, :] <= qpos[:, None]

        def probs(qi, ki):
            s = jnp.einsum('bhqd,bhkd->bhqk', qi, ki).astype(jnp.float32) * scale
            return jax.nn.softmax(jnp.where(causal, s, -jnp.inf), axis=-1)

        a = probs(q1i, k1) - lam_b * probs(q2i, k2)
        return jnp.einsum('bhqk,bhkd->bhqd', a.astype(v.dtype), v)

    out = lax.map(one_block, (q1b, q2b, jnp.arange(nqb)))
    return out.transpose(1, 2, 0, 3, 4).reshape(B, H, S, v.shape[-1])

def moba_attention(q, k, v):
    B, H, S, d = q.shape
    nb = -(-S // MOBA_BLOCK)
    pad = nb * MOBA_BLOCK - S
    kp = jnp.pad(k, ((0, 0), (0, 0), (0, pad), (0, 0)))
    vp = jnp.pad(v, ((0, 0), (0, 0), (0, pad), (0, 0)))
    kblk = kp.reshape(B, H, nb, MOBA_BLOCK, d)
    vblk = vp.reshape(B, H, nb, MOBA_BLOCK, d)
    kmean = kblk.mean(axis=3)
    n_sel = min(MOBA_TOPK, nb)
    nqc = S // MOBA_Q_CHUNK
    scale = d ** -0.5
    qc = q.reshape(B, H, nqc, MOBA_Q_CHUNK, d).transpose(2, 0, 1, 3, 4)
    blk_ids = jnp.arange(nb)
    bidx = jnp.arange(B)[:, None, None, None]
    hidx = jnp.arange(H)[None, :, None, None]

    def one_chunk(args):
        qi, ci = args
        q0 = ci * MOBA_Q_CHUNK
        own = q0 // MOBA_BLOCK
        qpos = q0 + jnp.arange(MOBA_Q_CHUNK)
        gate = jnp.einsum('bhqd,bhnd->bhqn', qi, kmean).astype(jnp.float32)
        gate = jnp.where(blk_ids < own, gate, -jnp.inf)
        _, gidx = lax.top_k(gate, n_sel)
        sel_valid = gidx < own
        ksel = kblk[bidx, hidx, gidx]
        vsel = vblk[bidx, hidx, gidx]
        s_sel = jnp.einsum('bhqd,bhqnkd->bhqnk', qi, ksel).astype(jnp.float32) * scale
        s_sel = jnp.where(sel_valid[..., None], s_sel, -jnp.inf)
        s_sel = s_sel.reshape(B, H, MOBA_Q_CHUNK, n_sel * MOBA_BLOCK)
        k_own = lax.dynamic_slice_in_dim(kp, own * MOBA_BLOCK, MOBA_BLOCK, axis=2)
        v_own = lax.dynamic_slice_in_dim(vp, own * MOBA_BLOCK, MOBA_BLOCK, axis=2)
        own_pos = own * MOBA_BLOCK + jnp.arange(MOBA_BLOCK)
        s_own = jnp.einsum('bhqd,bhkd->bhqk', qi, k_own).astype(jnp.float32) * scale
        s_own = jnp.where(own_pos[None, :] <= qpos[:, None], s_own, -jnp.inf)
        probs = jax.nn.softmax(jnp.concatenate([s_sel, s_own], axis=-1), axis=-1)
        p_sel = probs[..., :n_sel * MOBA_BLOCK].reshape(B, H, MOBA_Q_CHUNK, n_sel, MOBA_BLOCK)
        p_own = probs[..., n_sel * MOBA_BLOCK:]
        return (jnp.einsum('bhqnk,bhqnkd->bhqd', p_sel.astype(v.dtype), vsel)
                + jnp.einsum('bhqk,bhkd->bhqd', p_own.astype(v.dtype), v_own))

    out = lax.map(one_chunk, (qc, jnp.arange(nqc)))
    return out.transpose(1, 2, 0, 3, 4).reshape(B, H, S, d)

def even_mixer(u, w_in, w_out, lq1, lk1, lq2, lk2, subln_g, cos, sin, layer_idx):
    B, S, _ = u.shape
    proj = u @ w_in
    cuts = list(np.cumsum([SB_WIDTH, SB_WIDTH, SB_WIDTH, DIFF_QK_WIDTH, DIFF_QK_WIDTH]))
    a_q, a_k, a_v, b_q, b_k, b_v = jnp.split(proj, [int(c) for c in cuts], axis=-1)
    o_a = stick_breaking_attention(to_heads(a_q, SB_HEADS), to_heads(a_k, SB_HEADS),
                                   to_heads(a_v, SB_HEADS))
    bq = b_q.reshape(B, S, DIFF_HEADS, 2, DIFF_HEAD_DIM)
    bk = b_k.reshape(B, S, DIFF_HEADS, 2, DIFF_HEAD_DIM)
    rq = lambda t: apply_partial_rope(t, cos, sin).transpose(0, 2, 1, 3)
    q1, q2 = rq(bq[..., 0, :]), rq(bq[..., 1, :])
    k1, k2 = rq(bk[..., 0, :]), rq(bk[..., 1, :])
    lam_init = 0.8 - 0.6 * math.exp(-0.3 * layer_idx)
    f32 = jnp.float32
    lam = (jnp.exp(jnp.sum(lq1.astype(f32) * lk1.astype(f32), axis=-1))
           - jnp.exp(jnp.sum(lq2.astype(f32) * lk2.astype(f32), axis=-1)) + lam_init)
    o_b = diff_attention(q1, q2, k1, k2, to_heads(b_v, DIFF_HEADS), lam)
    o_b = rms_norm(o_b, subln_g) * (1.0 - lam_init)
    merged = jnp.concatenate([from_heads(o_a), from_heads(o_b)], axis=-1)
    return merged @ w_out

def odd_mixer(u, w_in, w_out, cos, sin):
    B, S, _ = u.shape
    q, k, v = jnp.split(u @ w_in, 3, axis=-1)
    q = apply_partial_rope(q.reshape(B, S, MOBA_HEADS, MOBA_HEAD_DIM), cos, sin).transpose(0, 2, 1, 3)
    k = apply_partial_rope(k.reshape(B, S, MOBA_HEADS, MOBA_HEAD_DIM), cos, sin).transpose(0, 2, 1, 3)
    o = moba_attention(q, k, to_heads(v, MOBA_HEADS))
    return from_heads(o) @ w_out

def squared_relu_mlp(u, w1, w2):
    return jnp.square(jax.nn.relu(u @ w1)) @ w2

def second_inputs(seed: int = 0) -> dict:
    key = jax.random.key(seed)
    ks = jax.random.split(key, 24)
    f32 = jnp.float32
    nrm = lambda k, shape, fan_in: jax.random.normal(k, shape, f32) * (fan_in ** -0.5)
    gain = lambda k, shape: 1.0 + 0.01 * jax.random.normal(k, shape, f32)
    x = jax.random.normal(ks[0], (BATCH, SEQ, D_MODEL), f32)
    p = jax.random.normal(ks[1], (DEPTH, BATCH, SEQ, PLE_DIM), f32)
    offsets = jax.random.randint(ks[2], (BATCH, 1), 0, 4096, dtype=jnp.int32)
    positions = (offsets + jnp.arange(SEQ, dtype=jnp.int32)[None, :]).astype(jnp.int32)
    return {
        "x": x,
        "p": p,
        "positions": positions,
        "attn_norm": gain(ks[3], (DEPTH, D_MODEL)),
        "ab_w_in": nrm(ks[4], (N_EVEN, D_MODEL, EVEN_IN_WIDTH), D_MODEL),
        "ab_w_out": nrm(ks[5], (N_EVEN, EVEN_OUT_WIDTH, D_MODEL), EVEN_OUT_WIDTH),
        "diff_lam_q1": 0.1 * jax.random.normal(ks[6], (N_EVEN, DIFF_HEADS, DIFF_HEAD_DIM), f32),
        "diff_lam_k1": 0.1 * jax.random.normal(ks[7], (N_EVEN, DIFF_HEADS, DIFF_HEAD_DIM), f32),
        "diff_lam_q2": 0.1 * jax.random.normal(ks[8], (N_EVEN, DIFF_HEADS, DIFF_HEAD_DIM), f32),
        "diff_lam_k2": 0.1 * jax.random.normal(ks[9], (N_EVEN, DIFF_HEADS, DIFF_HEAD_DIM), f32),
        "diff_subln": gain(ks[10], (N_EVEN, DIFF_V_DIM)),
        "moba_w_in": nrm(ks[11], (N_ODD, D_MODEL, 3 * MOBA_WIDTH), D_MODEL),
        "moba_w_out": nrm(ks[12], (N_ODD, MOBA_WIDTH, D_MODEL), MOBA_WIDTH),
        "mlp_norm": gain(ks[13], (DEPTH, D_MODEL)),
        "w_ff1": nrm(ks[14], (DEPTH, D_MODEL, D_FF_2), D_MODEL),
        "w_ff2": nrm(ks[15], (DEPTH, D_FF_2, D_MODEL), D_FF_2),
        "ple_norm": gain(ks[16], (DEPTH, D_MODEL)),
        "ple_gate": nrm(ks[17], (DEPTH, D_MODEL, D_MODEL), D_MODEL),
        "ple_proj": nrm(ks[18], (DEPTH, PLE_DIM, D_MODEL), PLE_DIM),
        "final_norm": gain(ks[19], (D_MODEL,)),
    }

def second_block(x, p, positions, attn_norm, ab_w_in, ab_w_out, diff_lam_q1, diff_lam_k1,
              diff_lam_q2, diff_lam_k2, diff_subln, moba_w_in, moba_w_out, mlp_norm,
              w_ff1, w_ff2, ple_norm, ple_gate, ple_proj, final_norm):
    cos, sin = rope_tables(positions, DIFF_HEAD_DIM)
    h = x
    for i in range(DEPTH):
        u = rms_norm(h, attn_norm[i])
        if i % 2 == 0:
            j = i // 2
            mix = even_mixer(u, ab_w_in[j], ab_w_out[j], diff_lam_q1[j], diff_lam_k1[j],
                             diff_lam_q2[j], diff_lam_k2[j], diff_subln[j], cos, sin, i)
        else:
            j = i // 2
            mix = odd_mixer(u, moba_w_in[j], moba_w_out[j], cos, sin)
        h = h + mix
        h = h + squared_relu_mlp(rms_norm(h, mlp_norm[i]), w_ff1[i], w_ff2[i])
        gate = jax.nn.sigmoid(rms_norm(h, ple_norm[i]) @ ple_gate[i])
        h = h + gate * (p[i].astype(h.dtype) @ ple_proj[i])
    return rms_norm(h, final_norm)


_first_inputs_2 = second_inputs


def second_inputs(seed=0):
    import zlib

    import numpy as np

    out = dict(_first_inputs_2(seed))
    spreads = {}
    factors = {}
    for name, (base, spread) in spreads.items():
        noise = np.random.default_rng([zlib.crc32(name.encode()), seed]).standard_normal(out[name].shape)
        drawn = base * np.exp(spread * noise) if base else spread * noise
        out[name] = __import__('jax').numpy.asarray(drawn.astype(out[name].dtype))
    for name, factor in factors.items():
        out[name] = (out[name] * factor).astype(out[name].dtype)
    return out


_narrow_inputs_2 = second_inputs


def second_inputs(seed=0):

    out = dict(_narrow_inputs_2(seed))
    wider = {'attn_norm': 6.73,
     'diff_subln': 11.32,
     'mlp_norm': 6.2,
     'ple_norm': 12.0,
     'final_norm': 6.4}
    for name, times in wider.items():
        mean = out[name].mean()
        out[name] = (mean + times * (out[name] - mean)).astype(out[name].dtype)
    return out


DEPTH_3 = 1

HG_HEADS = 8
HG_KDIM = 128
HG_VDIM = 128
HG_CHUNK = 64
HG_WIDTH_K = HG_HEADS * HG_KDIM
HG_WIDTH_V = HG_HEADS * HG_VDIM
MLA_HEADS = 8
MLA_Q_RANK = 384
MLA_KV_RANK = 256
MLA_NOPE = 128
MLA_ROPE = 64
MLA_VDIM = 128
MLA_QK_DIM = MLA_NOPE + MLA_ROPE
ROPE_THETA_3 = 10000.0
N_BRANCH = 2
IN_SPLITS = (HG_WIDTH_K, HG_WIDTH_K, HG_WIDTH_V, HG_WIDTH_V, MLA_Q_RANK, MLA_KV_RANK, MLA_ROPE, D_MODEL, D_MODEL)
IN_COLS = sum(IN_SPLITS)
N_GROUPS_3 = 8
EXPERTS_PER_GROUP = 8
N_EXPERTS = N_GROUPS_3 * EXPERTS_PER_GROUP
TOP_K_IN_GROUP = 2
EXPERT_FF = 512
MOE_BLOCK = 128


def rmsnorm_3(x, w):
    xf = x.astype(jnp.float32)
    y = xf * lax.rsqrt(jnp.mean(xf * xf, axis=-1, keepdims=True) + EPS)
    return (y * w.astype(jnp.float32)).astype(x.dtype)

def apply_rope(x, cos, sin):
    x1, x2 = jnp.split(x.astype(jnp.float32), 2, axis=-1)
    return jnp.concatenate([x1 * cos - x2 * sin, x2 * cos + x1 * sin], axis=-1).astype(x.dtype)

def hgrn2_mixer(q_raw, f_raw, i_raw, g_raw, lb, out_norm_w):
    B, S, _ = q_raw.shape
    n = S // HG_CHUNK
    f32 = jnp.float32
    q = jax.nn.silu(q_raw.astype(f32)) * (HG_KDIM ** -0.5)
    lbf = lb.astype(f32)
    fg = lbf + (1.0 - lbf) * jax.nn.sigmoid(f_raw.astype(f32))
    k = 1.0 - fg
    logf = jnp.log(fg)
    v = i_raw.astype(f32)

    def to_chunks(t, d):
        return t.reshape(B, n, HG_CHUNK, HG_HEADS, d).transpose(1, 0, 3, 2, 4)

    qc, kc, lfc = to_chunks(q, HG_KDIM), to_chunks(k, HG_KDIM), to_chunks(logf, HG_KDIM)
    vc = to_chunks(v, HG_VDIM)
    causal = jnp.tril(jnp.ones((HG_CHUNK, HG_CHUNK), dtype=bool))

    def step(state, inp):
        qt, kt, lft, vt = inp
        bcum = jnp.cumsum(lft, axis=2)
        diff = bcum[:, :, :, None, :] - bcum[:, :, None, :, :]
        decay = jnp.exp(jnp.where(causal[None, None, :, :, None], diff, -jnp.inf))
        attn = jnp.sum(qt[:, :, :, None, :] * kt[:, :, None, :, :] * decay, axis=-1)
        o = jnp.einsum('bhts,bhsv->bhtv', attn, vt) + \
            jnp.einsum('bhtk,bhkv->bhtv', qt * jnp.exp(bcum), state)
        b_last = bcum[:, :, -1]
        k_dec = kt * jnp.exp(b_last[:, :, None, :] - bcum)
        state = jnp.exp(b_last)[..., None] * state + jnp.einsum('bhsk,bhsv->bhkv', k_dec, vt)
        return state, o

    s0 = jnp.zeros((B, HG_HEADS, HG_KDIM, HG_VDIM), f32)
    _, o = lax.scan(step, s0, (qc, kc, lfc, vc))
    o = o.transpose(1, 0, 3, 2, 4).reshape(B, S, HG_HEADS, HG_VDIM)
    o = rmsnorm_3(o, out_norm_w).reshape(B, S, HG_WIDTH_V)
    g = g_raw.astype(f32)
    return o * jax.nn.silu(g)

def mla_mixer(c_q, c_kv, k_rope_raw, positions, q_norm_w, w_uq, kv_norm_w, w_ukv):
    B, S, _ = c_q.shape
    half = MLA_ROPE // 2
    inv_freq = ROPE_THETA_3 ** (-jnp.arange(half, dtype=jnp.float32) / half)
    ang = positions.astype(jnp.float32)[..., None] * inv_freq
    cos, sin = jnp.cos(ang), jnp.sin(ang)

    q = (rmsnorm_3(c_q, q_norm_w) @ w_uq).reshape(B, S, MLA_HEADS, MLA_QK_DIM)
    q_nope, q_pe = q[..., :MLA_NOPE], q[..., MLA_NOPE:]
    q_pe = apply_rope(q_pe, cos[:, :, None, :], sin[:, :, None, :])
    kv = (rmsnorm_3(c_kv, kv_norm_w) @ w_ukv).reshape(B, S, MLA_HEADS, MLA_NOPE + MLA_VDIM)
    k_nope, v = kv[..., :MLA_NOPE], kv[..., MLA_NOPE:]
    k_pe = apply_rope(k_rope_raw, cos, sin)
    k = jnp.concatenate([k_nope, jnp.broadcast_to(k_pe[:, :, None, :], (B, S, MLA_HEADS, MLA_ROPE))], axis=-1)
    qf = jnp.concatenate([q_nope, q_pe], axis=-1) * (MLA_QK_DIM ** -0.5)

    nq = S // Q_BLOCK
    qb = qf.reshape(B, nq, Q_BLOCK, MLA_HEADS, MLA_QK_DIM).transpose(1, 0, 3, 2, 4)
    kpos = jnp.arange(S)

    def attend(args):
        qblk, blk = args
        s = jnp.einsum('bhqd,bkhd->bhqk', qblk, k, preferred_element_type=jnp.float32)
        qpos = blk * Q_BLOCK + jnp.arange(Q_BLOCK)
        s = jnp.where(kpos[None, :] <= qpos[:, None], s, -jnp.inf)
        p = jax.nn.softmax(s, axis=-1)
        return jnp.einsum('bhqk,bkhd->bqhd', p.astype(v.dtype), v)

    o = lax.map(attend, (qb, jnp.arange(nq)))
    return o.transpose(1, 0, 2, 3, 4).reshape(B, S, MLA_HEADS * MLA_VDIM)

def hierarchical_moe(h, w_group, b_group, w_expert, b_expert, w1, w3, w2):
    B, S, D = h.shape
    T = B * S
    xt = h.reshape(T, D)
    g_prob = jax.nn.softmax((xt @ w_group).astype(jnp.float32) + b_group.astype(jnp.float32), axis=-1)
    g_w, g_idx = lax.top_k(g_prob, 1)
    e_logits = ((xt @ w_expert).astype(jnp.float32) + b_expert.astype(jnp.float32)).reshape(T, N_GROUPS_3, EXPERTS_PER_GROUP)
    e_sel = jnp.take_along_axis(e_logits, g_idx[:, :, None], axis=1)[:, 0]
    e_prob = jax.nn.softmax(e_sel, axis=-1)
    e_w, e_idx = lax.top_k(e_prob, TOP_K_IN_GROUP)
    e_w = e_w / jnp.sum(e_w, axis=-1, keepdims=True)
    weights = g_w * e_w
    expert_ids = g_idx * EXPERTS_PER_GROUP + e_idx

    A = T * TOP_K_IN_GROUP
    flat_e = expert_ids.reshape(A)
    flat_t = jnp.repeat(jnp.arange(T, dtype=jnp.int32), TOP_K_IN_GROUP)
    flat_w = weights.reshape(A)
    order = jnp.argsort(flat_e)
    se, st, sw = flat_e[order], flat_t[order], flat_w[order]
    counts = jax.ops.segment_sum(jnp.ones_like(se), se, num_segments=N_EXPERTS)
    starts = jnp.cumsum(counts) - counts
    padded = (counts + MOE_BLOCK - 1) // MOE_BLOCK * MOE_BLOCK
    pends = jnp.cumsum(padded)
    pstarts = pends - padded
    dest = pstarts[se] + (jnp.arange(A, dtype=se.dtype) - starts[se])
    n_blocks = A // MOE_BLOCK + N_EXPERTS
    cap = n_blocks * MOE_BLOCK
    tok_buf = jnp.full((cap,), T, dtype=jnp.int32).at[dest].set(st)
    w_buf = jnp.zeros((cap,), jnp.float32).at[dest].set(sw)
    block_start = jnp.arange(n_blocks, dtype=pends.dtype) * MOE_BLOCK
    block_expert = jnp.minimum(jnp.searchsorted(pends, block_start, side='right'), N_EXPERTS - 1)
    x_pad = jnp.concatenate([xt, jnp.zeros((1, D), xt.dtype)], axis=0)

    def run_block(args):
        toks, wts, e = args
        xb = x_pad[toks]
        hid = jax.nn.silu(xb @ w1[e]) * (xb @ w3[e])
        return (hid @ w2[e]) * wts[:, None].astype(xb.dtype)

    yb = lax.map(run_block, (tok_buf.reshape(n_blocks, MOE_BLOCK), w_buf.reshape(n_blocks, MOE_BLOCK), block_expert))
    out = jax.ops.segment_sum(yb.reshape(cap, D), tok_buf, num_segments=T + 1)[:T]
    return out.reshape(B, S, D)

def third_inputs(seed: int = 0) -> dict:
    key = jax.random.key(seed)
    ks = jax.random.split(key, 24)
    f32 = jnp.float32
    nrm = lambda k, shape, scale: jax.random.normal(k, shape, f32) * scale
    gain = lambda k, shape: 1.0 + 0.02 * jax.random.normal(k, shape, f32)
    x = jax.random.normal(ks[0], (BATCH, SEQ, D_MODEL), f32)
    offsets = jax.random.randint(ks[1], (BATCH, 1), 0, 4096, dtype=jnp.int32)
    positions = offsets + jnp.arange(SEQ, dtype=jnp.int32)[None, :]
    return {
        "x": x,
        "positions": positions,
        "attn_norm_w": gain(ks[2], (DEPTH_3, D_MODEL)),
        "w_in": nrm(ks[3], (DEPTH_3, D_MODEL, IN_COLS), D_MODEL ** -0.5),
        "hg_lower_bound": nrm(ks[4], (DEPTH_3 + 1, HG_WIDTH_K), 0.5),
        "hg_out_norm_w": gain(ks[5], (DEPTH_3, HG_VDIM)),
        "mla_q_norm_w": gain(ks[6], (DEPTH_3, MLA_Q_RANK)),
        "mla_w_uq": nrm(ks[7], (DEPTH_3, MLA_Q_RANK, MLA_HEADS * MLA_QK_DIM), MLA_Q_RANK ** -0.5),
        "mla_kv_norm_w": gain(ks[8], (DEPTH_3, MLA_KV_RANK)),
        "mla_w_ukv": nrm(ks[9], (DEPTH_3, MLA_KV_RANK, MLA_HEADS * (MLA_NOPE + MLA_VDIM)), MLA_KV_RANK ** -0.5),
        "w_branch_hgrn": nrm(ks[10], (DEPTH_3, HG_WIDTH_V, D_MODEL), HG_WIDTH_V ** -0.5),
        "w_branch_mla": nrm(ks[11], (DEPTH_3, MLA_HEADS * MLA_VDIM, D_MODEL), (MLA_HEADS * MLA_VDIM) ** -0.5),
        "w_out": nrm(ks[12], (DEPTH_3, D_MODEL, D_MODEL), D_MODEL ** -0.5),
        "ffn_norm_w": gain(ks[13], (DEPTH_3, D_MODEL)),
        "router_group_w": nrm(ks[14], (DEPTH_3, D_MODEL, N_GROUPS_3), D_MODEL ** -0.5),
        "router_group_b": nrm(ks[15], (DEPTH_3, N_GROUPS_3), 0.01),
        "router_expert_w": nrm(ks[16], (DEPTH_3, D_MODEL, N_EXPERTS), D_MODEL ** -0.5),
        "router_expert_b": nrm(ks[17], (DEPTH_3, N_EXPERTS), 0.01),
        "expert_w1": nrm(ks[18], (DEPTH_3, N_EXPERTS, D_MODEL, EXPERT_FF), D_MODEL ** -0.5),
        "expert_w3": nrm(ks[19], (DEPTH_3, N_EXPERTS, D_MODEL, EXPERT_FF), D_MODEL ** -0.5),
        "expert_w2": nrm(ks[20], (DEPTH_3, N_EXPERTS, EXPERT_FF, D_MODEL), EXPERT_FF ** -0.5),
        "final_norm_w": gain(ks[21], (D_MODEL,)),
    }

def third_block(x, positions, attn_norm_w, w_in, hg_lower_bound, hg_out_norm_w, mla_q_norm_w, mla_w_uq,
              mla_kv_norm_w, mla_w_ukv, w_branch_hgrn, w_branch_mla, w_out, ffn_norm_w, router_group_w,
              router_group_b, router_expert_w, router_expert_b, expert_w1, expert_w3, expert_w2, final_norm_w):
    split_idx = [int(v) for v in np.cumsum(IN_SPLITS)[:-1]]
    lb_all = jnp.cumsum(jax.nn.softmax(hg_lower_bound.astype(jnp.float32), axis=0), axis=0)
    for l in range(DEPTH_3):
        h = rmsnorm_3(x, attn_norm_w[l])
        z = h @ w_in[l]
        hq, hf, hi, hg, cq, ckv, kr, gate_a, gate_b = jnp.split(z, split_idx, axis=-1)
        o_a = hgrn2_mixer(hq, hf, hi, hg, lb_all[l], hg_out_norm_w[l]).astype(x.dtype)
        o_b = mla_mixer(cq, ckv, kr, positions, mla_q_norm_w[l], mla_w_uq[l], mla_kv_norm_w[l], mla_w_ukv[l])
        y = jax.nn.sigmoid(gate_a) * (o_a @ w_branch_hgrn[l]) + jax.nn.sigmoid(gate_b) * (o_b @ w_branch_mla[l])
        x = x + y @ w_out[l]
        h = rmsnorm_3(x, ffn_norm_w[l])
        x = x + hierarchical_moe(h, router_group_w[l], router_group_b[l], router_expert_w[l], router_expert_b[l],
                                 expert_w1[l], expert_w3[l], expert_w2[l])
    return rmsnorm_3(x, final_norm_w)


def setup_inputs(seed=0):
    out = dict(first_inputs(seed))
    for name, value in second_inputs(seed + 1).items():
        if name != "x":
            out[name + "_2"] = value
    for name, value in third_inputs(seed + 2).items():
        if name != "x":
            out[name + "_3"] = value
    return out


def reference(
    x, mem, norm_g, ssm_in_w, ssm_conv_w, ssm_conv_b, ssm_dt_bias, ssm_A_log, ssm_D, ssm_norm_g,
    ssm_out_w, cf_pw1_w, cf_pw1_b, cf_dw_w, cf_dw_b, cf_ln_g, cf_ln_b, cf_pw2_w, cf_pw2_b,
    xa_mem_g, xa_q_w, xa_kv_w, xa_o_w, ffn_in_w, ffn_conv_w, ffn_conv_b, ffn_out_w, p_2,
    positions_2, attn_norm_2, ab_w_in_2, ab_w_out_2, diff_lam_q1_2, diff_lam_k1_2,
    diff_lam_q2_2, diff_lam_k2_2, diff_subln_2, moba_w_in_2, moba_w_out_2, mlp_norm_2, w_ff1_2,
    w_ff2_2, ple_norm_2, ple_gate_2, ple_proj_2, final_norm_2, positions_3, attn_norm_w_3,
    w_in_3, hg_lower_bound_3, hg_out_norm_w_3, mla_q_norm_w_3, mla_w_uq_3, mla_kv_norm_w_3,
    mla_w_ukv_3, w_branch_hgrn_3, w_branch_mla_3, w_out_3, ffn_norm_w_3, router_group_w_3,
    router_group_b_3, router_expert_w_3, router_expert_b_3, expert_w1_3, expert_w3_3,
    expert_w2_3, final_norm_w_3,
):
    x = first_block(
        x, mem, norm_g, ssm_in_w, ssm_conv_w, ssm_conv_b, ssm_dt_bias, ssm_A_log, ssm_D,
        ssm_norm_g, ssm_out_w, cf_pw1_w, cf_pw1_b, cf_dw_w, cf_dw_b, cf_ln_g, cf_ln_b, cf_pw2_w,
        cf_pw2_b, xa_mem_g, xa_q_w, xa_kv_w, xa_o_w, ffn_in_w, ffn_conv_w, ffn_conv_b,
        ffn_out_w,
    )
    x = second_block(
        x, p_2, positions_2, attn_norm_2, ab_w_in_2, ab_w_out_2, diff_lam_q1_2, diff_lam_k1_2,
        diff_lam_q2_2, diff_lam_k2_2, diff_subln_2, moba_w_in_2, moba_w_out_2, mlp_norm_2,
        w_ff1_2, w_ff2_2, ple_norm_2, ple_gate_2, ple_proj_2, final_norm_2,
    )
    return third_block(
        x, positions_3, attn_norm_w_3, w_in_3, hg_lower_bound_3, hg_out_norm_w_3,
        mla_q_norm_w_3, mla_w_uq_3, mla_kv_norm_w_3, mla_w_ukv_3, w_branch_hgrn_3,
        w_branch_mla_3, w_out_3, ffn_norm_w_3, router_group_w_3, router_group_b_3,
        router_expert_w_3, router_expert_b_3, expert_w1_3, expert_w3_3, expert_w2_3,
        final_norm_w_3,
    )


_drawn_inputs = setup_inputs


def setup_inputs(seed=0):
    import zlib

    import numpy as np

    out = dict(_drawn_inputs(seed))
    spreads = {}
    factors = {'diff_lam_q1_2': 3.185,
     'diff_lam_k1_2': 2.752,
     'diff_lam_q2_2': 4.681,
     'diff_lam_k2_2': 3.238,
     'ple_norm_2': 2.827,
     'attn_norm_w_3': 4.043,
     'hg_lower_bound_3': 3.491,
     'hg_out_norm_w_3': 5.549,
     'mla_q_norm_w_3': 8.0,
     'mla_kv_norm_w_3': 8.0,
     'ffn_norm_w_3': 3.725,
     'router_group_b_3': 31.192,
     'router_expert_b_3': 8.0,
     'final_norm_w_3': 7.839}
    for name, (base, spread) in spreads.items():
        noise = np.random.default_rng([zlib.crc32(name.encode()), seed]).standard_normal(out[name].shape)
        drawn = base * np.exp(spread * noise) if base else spread * noise
        out[name] = __import__('jax').numpy.asarray(drawn.astype(out[name].dtype))
    for name, factor in factors.items():
        out[name] = (out[name] * factor).astype(out[name].dtype)
    return out
```

```python
import math
from contextlib import ExitStack

import numpy as np
import concourse.bass as bass
from concourse import mybir

F32 = mybir.dt.float32
I32 = mybir.dt.int32
ACT = mybir.ActivationFunctionType
ALU = mybir.AluOpType
AX = mybir.AxisListType

P = 128
T = 256
D = 1024
DC = D // P
EPS = 1e-6
SLOTS = 12
UNIT = 8 * T
NB = 4
ARENA = 76
DFF = 2816
FC = DFF // P
NEXP = 64
EFF = 512
SSM_HEADS, HPG, SSM_P = 32, 8, 64
CF_K = 31
BIG = 1e30

LINEARS = [
    ("ssm_x", 8, 12, 1), ("ssm_z", 8, 8, 1), ("ssm_out", 16, 4, 1),
    ("xa_k0", 8, 4, 1), ("xa_v0", 8, 4, 1), ("xa_q0", 8, 4, 1), ("xa_o0", 8, 4, 1),
    ("ffn_in0", 8, 22, 1), ("ffn_out0", 22, 4, 1),
    ("pw1", 8, 8, 1), ("pw2", 8, 4, 1),
    ("xa_k1", 8, 4, 1), ("xa_v1", 8, 4, 1), ("xa_q1", 8, 4, 1), ("xa_o1", 8, 4, 1),
    ("ffn_in1", 8, 22, 1), ("ffn_out1", 22, 4, 1),
    ("ab_aq", 8, 2, 1), ("ab_ak", 8, 2, 1), ("ab_av", 8, 2, 1),
    ("ab_bq", 8, 2, 1), ("ab_bk", 8, 2, 1), ("ab_bv", 8, 2, 1), ("ab_out", 8, 4, 1),
    ("ff1_0", 8, 16, 1), ("ff2_0", 32, 4, 1), ("gate0", 8, 4, 1), ("proj0", 2, 4, 4),
    ("mb_q", 8, 4, 1), ("mb_k", 8, 4, 1), ("mb_v", 8, 4, 1), ("mb_out", 8, 4, 1),
    ("ff1_1", 8, 16, 1), ("ff2_1", 32, 4, 1), ("gate1", 8, 4, 1), ("proj1", 2, 4, 4),
    ("hq", 8, 4, 1), ("hf", 8, 4, 1), ("hi", 8, 4, 1), ("hg", 8, 4, 1), ("lat", 8, 3, 1),
    ("uqn", 3, 4, 2), ("uqr", 3, 2, 2), ("uk", 2, 4, 4), ("uv", 2, 4, 4),
    ("ga", 8, 4, 1), ("bra", 8, 4, 1), ("gb", 8, 4, 1), ("brb", 8, 4, 1), ("wout", 8, 4, 1),
]
LIN = {}
_unit = _pair = 0
for _name, _kc, _pairs, _share in LINEARS:
    LIN[_name] = (_kc, _pairs, _share, _unit, _pair)
    _unit += -(-_pairs // _share) * -(-_kc // 8)
    _pair += _pairs
DENSE_UNITS = _unit
EXPERT_UNITS = 6
UNITS = DENSE_UNITS + NEXP * EXPERT_UNITS

VEC = {}
_at = 0
for _name, _n in [
    ("norm_g", 96), ("ssm_cw", 4 * 24), ("ssm_cb", 24), ("ssm_D", 16), ("ssm_ng", 16),
    ("pw1_b", 16), ("dw_w", CF_K * 8), ("dw_b", 8), ("ln_g", 8), ("ln_b", 8), ("pw2_b", 8),
    ("mem_g", 16), ("ffn_cw", 2 * 3 * 44), ("ffn_cb", 2 * 44),
    ("attn2", 16), ("lam", 16), ("subln", 1), ("mlp2", 16), ("ple2", 16), ("final2", 8),
    ("attn3", 8), ("hg_lb", 16), ("hg_on", 1), ("mla_qn", 3), ("mla_kn", 2), ("ffn3", 8), ("final3", 8),
    ("dt_b", 32), ("A_log", 32), ("inv2", 1), ("inv3", 1),
]:
    VEC[_name] = _at
    _at += _n
NVEC = _at

CON = {"ident": 0, "ones": 128, "upto": 256, "from": 384, "rot2": 512, "rot3": 640, "cmask": 768, "iota": 1152}
NCON = 1152 + 64

NORMS = [("b1_0_in", 8), ("ssm", 16), ("b1_0_mix", 8), ("mem0", 8), ("xa_in0", 8), ("xa_out0", 8),
         ("ff_in0", 8), ("ff_out0", 8),
         ("b1_1_in", 8), ("ln", 8), ("b1_1_mix", 8), ("mem1", 8), ("xa_in1", 8), ("xa_out1", 8),
         ("ff_in1", 8), ("ff_out1", 8),
         ("b2_0_in", 8), ("mlp0", 8), ("ple0", 8), ("b2_1_in", 8), ("mlp1", 8), ("ple1", 8), ("final2", 8),
         ("b3_in", 8), ("qn", 3), ("kn", 2), ("ffn3", 8), ("final3", 8)]
NORM = {}
_at = 0
for _i, (_name, _n) in enumerate(NORMS):
    NORM[_name] = (_i, _n, _at)
    _at += _n
LOADS = ["wdt", "mem0", "mem1", "pos2", "strict", "p0", "p1", "levels", "pos3", "router"]
BARRIERS = 4


def unit_of(name, p, kc):
    chunks, _, share, unit, _ = LIN[name]
    return unit + p // share * -(-chunks // 8) + kc // 8


def units_done(name, p):
    return unit_of(name, p, LIN[name][0] - 1) + 1


def pair_of(name, p):
    return LIN[name][4] + p


class Own:

    def __init__(self, eng, sem):
        self.eng, self.sem, self.n = eng, sem, 0

    def __call__(self, ins):
        self.n += 1
        ins.then_inc(self.sem, 1)

    def wait(self):
        self.eng.wait_ge(self.sem, self.n)


SEMS = """unit_used vec_in x_in aux_in phase_done own_act own_dve own_pool
sq_ready stat_ready var_ready std_ready r_ready normed x_ready
dt_mm dt_abs dt_ln dt_ready dta_ready conv_base xbc_ready cs_mm
cb_mm cbm_ready bt_mm btok_ready dte_in dte_ready xt_mm xdt_ready xde_ready st_mm st_ready
cr_mm seg_ready ecs_ready e_ready g_ready cp_ready y_mm y_ready gy_dve gy_pool
sc_mm s_read smax_ready exp_done p_ready pt_mm pts_ready o_mm o_evac
sg_ready ff_ready cv_base cv_ready mean_mm centered ln_out
ang_ready sincos rot_mm rs_ready rope_done
z_mm zabs_ready zln_ready spm_ready rs_mm rs_read wexp_ready sw_ready so_mm so_evac
lam_in lam_mm lam_exp lam_ready
hn_sq hn_stat hn_var hn_std hn_r hn_out
kf_ready b_ready d_ready lev_exp q_side k_side lev_mm lev_taken att_ready ho_mm ho_evac oa_ready
lb_ready lbs hg_sig hg_fg sq_q
rt_mm rt_log rt_exp wt_ready up_mm up_act up_taken dn_taken tr_mm x_done out_written
rank_mm fits_ready acc_zero zero_in htok_mm htok_ready gsel_ready gwsel_ready gather_mm xc_ready spread_mm spread_ready
silu_ready hid_ready y_out scattered""".split()


def program(nc, io):
    with ExitStack() as ctx:
        def sb(name, shape, dt=F32):
            return ctx.enter_context(nc.sbuf_tensor(name, shape, dt))

        W = sb("weight_ring", [P, SLOTS, 8, T])
        X = sb("residual", [P, DC, T])
        H = sb("normed_residual", [P, DC, T])
        A = sb("arena", [P, ARENA, T])
        VT = sb("vectors", [P, NVEC])
        CT = sb("constants", [P, NCON])
        VAR = sb("var", [P, T])
        STD = sb("std", [P, T])
        R = sb("rstd", [P, T])
        COS = sb("cos", [P, T])
        SIN = sb("sin", [P, T])
        SC = sb("small", [P, 384])
        PB = [ctx.enter_context(nc.psum_tensor(f"bank{b}", [P, 512], F32)) for b in range(8)]
        sem = {n: ctx.enter_context(nc.semaphore(n)) for n in SEMS}
        arrived = [ctx.enter_context(nc.semaphore(f"arrived{s}")) for s in range(SLOTS)]
        evac = [ctx.enter_context(nc.semaphore(f"evac{b}")) for b in range(NB)]

        ones = CT[:, CON["ones"]:CON["ones"] + P]
        ident = CT[:, CON["ident"]:CON["ident"] + P]
        upto = CT[:, CON["upto"]:CON["upto"] + P]
        onward = CT[:, CON["from"]:CON["from"] + P]
        rot2 = CT[:, CON["rot2"]:CON["rot2"] + P]
        rot3 = CT[:, CON["rot3"]:CON["rot3"] + P]
        cmask = CT[:, CON["cmask"]:CON["cmask"] + 384]
        STAT = PB[7][:, 0:T]

        def vec(name, i, n=1):
            return VT[:, VEC[name] + i:VEC[name] + i + n]

        def flat(a, n):
            return A[:, a:a + n, :].rearrange("p c t -> p (c t)")

        def tiles(base):
            return lambda t: A[:, base + t, :]

        def bank(b):
            return PB[b][:, :].rearrange("p (m t) -> p m t", m=2)

        xt = lambda t: X[:, t, :]
        ht = lambda t: H[:, t, :]
        MIX, SQ, SM, PTS = 48, 56, 40, 72
        mix = tiles(MIX)

        def wait_evac(eng, name, p):
            g = pair_of(name, p)
            eng.wait_ge(evac[g % NB], g // NB + 1)

        def wait_pair(eng, name, p):
            eng.wait_ge(sem["unit_used"], units_done(name, p))
            return pair_of(name, p) % NB

        phases = {"pe": 0, "act": 0, "dve": 0, "pool": 0}

        def meet(who, eng):
            eng.drain().then_inc(sem["phase_done"], 1)
            phases[who] += 1
            eng.wait_ge(sem["phase_done"], BARRIERS * phases[who])

        def linear_pe(pe, name, src, tokens=False, ready=None):
            chunks, pairs, share, _, _ = LIN[name]
            seen = set()
            for p in range(pairs):
                g = pair_of(name, p)
                b = g % NB
                if g >= NB:
                    pe.wait_ge(evac[b], g // NB)
                for m in range(2):
                    for kc in range(chunks):
                        u = unit_of(name, p, kc)
                        if u not in seen:
                            seen.add(u)
                            pe.wait_ge(arrived[u % SLOTS], 16 * (u // SLOTS + 1))
                        if ready and p == 0 and m == 0:
                            ready(pe, kc)
                        if share == 1:
                            w = W[:, u % SLOTS, kc % 8, :]
                        else:
                            w = W[:, u % SLOTS, p % share * chunks + kc, :]
                        half = slice(m * P, m * P + P)
                        l, r = (src(kc)[:, half], w) if tokens else (w[:, half], src(kc))
                        mm = nc.tensor.matmul(PB[b][:, m * T:m * T + T], l, r, start=(kc == 0), stop=(kc == chunks - 1))
                        if m == 1 and (kc % 8 == 7 or kc == chunks - 1) and (p % share == share - 1 or p == pairs - 1):
                            mm.then_inc(sem["unit_used"], 1)

        def norm_pe(pe, name):
            i, n, at = NORM[name]
            for t in range(n):
                pe.wait_ge(sem["sq_ready"], at + t + 1)
                mm = nc.tensor.matmul(STAT, ones, A[:, SQ + t, :], start=(t == 0), stop=(t == n - 1))
            mm.then_inc(sem["stat_ready"], 1)

        def norm_act(act, name, src, ready=None):
            i, n, at = NORM[name]
            for t in range(n):
                if ready:
                    ready(act, t)
                nc.scalar.activation(A[:, SQ + t, :], src(t), ACT.Square).then_inc(sem["sq_ready"], 1)
            act.wait_ge(sem["var_ready"], i + 1)
            nc.scalar.activation(STD[:, :], VAR[:, :], ACT.Sqrt).then_inc(sem["std_ready"], 1)

        def norm_dve(dve, name, src, gain, dst):
            i, n, at = NORM[name]
            dve.wait_ge(sem["stat_ready"], i + 1)
            nc.vector.tensor_scalar(VAR[:, :], STAT, 1.0 / (n * P), EPS, ALU.mult, ALU.add).then_inc(sem["var_ready"], 1)
            dve.wait_ge(sem["std_ready"], i + 1)
            nc.vector.reciprocal(R[:, :], STD[:, :]).then_inc(sem["r_ready"], 1)
            dve.wait_ge(sem["r_ready"], i + 1)
            for t in range(n):
                nc.vector.scalar_tensor_tensor(out=dst(t), in0=src(t), scalar=gain(t), in1=R[:, :],
                                               op0=ALU.mult, op1=ALU.mult).then_inc(sem["normed"], 1)

        def normed_ready(name):
            return lambda eng, kc: eng.wait_ge(sem["normed"], NORM[name][2] + kc + 1)

        def residual_pool(pool, name, k):
            for t in range(DC):
                pool.wait_ge(sem["normed"], NORM[name][2] + t + 1)
                nc.gpsimd.tensor_tensor(xt(t), xt(t), mix(t), ALU.add).then_inc(sem["x_ready"], 1)

        def x_after(k):
            return lambda eng, t: eng.wait_ge(sem["x_ready"], DC * k + t + 1)

        def copy_out_act(act, name, base, func=ACT.Identity, tokens=0):
            for p in range(LIN[name][1]):
                b = wait_pair(act, name, p)
                if tokens:
                    dst = flat(base, 2 * tokens // T).rearrange("p (m n) -> p m n", m=2)[:, :, p * T:p * T + T]
                else:
                    dst = A[:, base + 2 * p:base + 2 * p + 2, :]
                nc.scalar.activation(dst, bank(b), func).then_inc(evac[b], 1)

        def attend_pe(pe, heads, a0, b0, comps, causal, scores, pv):
            for i in range(heads + 2):
                if i < heads:
                    for c in range(comps):
                        a = a0 + i * comps + c
                        if a >= 2:
                            pe.wait_ge(sem["s_read"], a - 1)
                        scores(i, c, PB[4 + a % 2]).then_inc(sem["sc_mm"], 1)
                if 1 <= i <= heads:
                    b = b0 + i - 1
                    a = a0 + i * comps - 1
                    pr = flat(SM + 2 * (a % 4), 2)
                    pe.wait_ge(sem["p_ready"], b + 1)
                    if b >= 2:
                        pe.wait_ge(sem["pts_ready"], b - 1)
                    if causal:
                        blocks = [(0, 0), (P, P), (2 * P, 2 * P)]
                    else:
                        blocks = [(0, 0), (T, P), (P, T), (T + P, T + P)]
                    for src, dst in blocks:
                        mm = nc.tensor.transpose(PB[6 + b % 2][:, dst:dst + P], pr[:, src:src + P], ident)
                    mm.then_inc(sem["pt_mm"], 1)
                if i >= 2:
                    b = b0 + i - 2
                    pe.wait_ge(sem["pts_ready"], b + 1)
                    if b >= 2:
                        pe.wait_ge(sem["o_evac"], b - 1)
                    pv(i - 2, flat(PTS + 2 * (b % 2), 2), PB[2 + b % 2]).then_inc(sem["o_mm"], 1)

        def attend_act(act, heads, a0, b0, comps, causal, out):
            segs = [(0, P), (P, 384)] if causal else [(0, T), (T, 512)]
            for i in range(heads + 2):
                if i < heads:
                    for c in range(comps):
                        a = a0 + i * comps + c
                        act.wait_ge(sem["smax_ready"], a + 1)
                        s = flat(SM + 2 * (a % 4), 2)
                        for k, (lo, hi) in enumerate(segs):
                            j = 2 * (a % 4) + k
                            e = nc.scalar.activation(s[:, lo:hi], s[:, lo:hi], ACT.Exp, bias=SC[:, j:j + 1],
                                                     accum_out=SC[:, 8 + j:9 + j])
                        e.then_inc(sem["exp_done"], 1)
                if 1 <= i <= heads:
                    b = b0 + i - 1
                    act.wait_ge(sem["pt_mm"], b + 1)
                    if b >= 2:
                        act.wait_ge(sem["o_mm"], b - 1)
                    n = 384 if causal else 512
                    nc.scalar.activation(flat(PTS + 2 * (b % 2), 2)[:, 0:n], PB[6 + b % 2][:, 0:n],
                                         ACT.Identity).then_inc(sem["pts_ready"], 1)
                if i >= 2:
                    b = b0 + i - 2
                    act.wait_ge(sem["o_mm"], b + 1)
                    dst, src = out(i - 2, PB[2 + b % 2])
                    nc.scalar.activation(dst, src, ACT.Identity).then_inc(sem["o_evac"], 1)

        def attend_dve(dve, own, heads, a0, b0, comps, causal, scale, lam=None):
            segs = [(0, P), (P, 384)] if causal else [(0, T), (T, 512)]
            n = segs[1][1]
            for i in range(heads + 1):
                if i < heads:
                    for c in range(comps):
                        a = a0 + i * comps + c
                        s = flat(SM + 2 * (a % 4), 2)
                        dve.wait_ge(sem["sc_mm"], a + 1)
                        deep = 4 // comps
                        b = b0 + i
                        if b >= deep:
                            dve.wait_ge(sem["pt_mm"], b - deep + 1)
                        if causal:
                            ins = nc.vector.scalar_tensor_tensor(out=s[:, 0:n], in0=PB[4 + a % 2][:, 0:n], scalar=scale,
                                                                 in1=cmask, op0=ALU.mult, op1=ALU.add)
                        else:
                            ins = nc.vector.tensor_scalar(s[:, 0:n], PB[4 + a % 2][:, 0:n], scale, None, ALU.mult)
                        ins.then_inc(sem["s_read"], 1)
                        dve.wait_ge(sem["s_read"], a + 1)
                        for k, (lo, hi) in enumerate(segs):
                            j = 2 * (a % 4) + k
                            m = nc.vector.tensor_reduce(SC[:, j:j + 1], s[:, lo:hi], AX.X, ALU.max, negate=True)
                        m.then_inc(sem["smax_ready"], 1)
                if i >= 1:
                    h = i - 1
                    for c in range(comps):
                        a = a0 + h * comps + c
                        s = flat(SM + 2 * (a % 4), 2)
                        j = 8 + 2 * (a % 4)
                        dve.wait_ge(sem["exp_done"], a + 1)
                        own(nc.vector.reciprocal(SC[:, j + 8:j + 10], SC[:, j:j + 2]))
                        own.wait()
                        if lam is not None and c == 1:
                            own(nc.vector.tensor_scalar(SC[:, j + 8:j + 10], SC[:, j + 8:j + 10], lam(h), -1.0,
                                                        ALU.mult, ALU.mult))
                            own.wait()
                        for k, (lo, hi) in enumerate(segs):
                            r = SC[:, j + 8 + k:j + 9 + k]
                            if c == 0:
                                ins = nc.vector.tensor_scalar(s[:, lo:hi], s[:, lo:hi], r, None, ALU.mult)
                            else:
                                s0 = flat(SM + 2 * ((a - 1) % 4), 2)
                                ins = nc.vector.scalar_tensor_tensor(out=s[:, lo:hi], in0=s[:, lo:hi], scalar=r,
                                                                     in1=s0[:, lo:hi], op0=ALU.mult, op1=ALU.add)
                            if c < comps - 1 and k == 1:
                                own(ins)
                        if c < comps - 1:
                            own.wait()
                    ins.then_inc(sem["p_ready"], 1)

        def pv_causal(values, rows):
            def pv(h, pt, out):
                o = out[rows(h), 0:T]
                nc.tensor.matmul(o, values(h, 0), pt[:, 0:T], start=True, stop=False)
                return nc.tensor.matmul(o[:, P:T], values(h, 1), pt[:, T:T + P], start=False, stop=True)
            return pv

        def scores_causal(parts):
            def scores(h, c, out):
                ps = parts(h, c)
                for lo, hi, q, k in ((0, P, 0, P), (P, 384, P, T)):
                    for n, (qs, ks) in enumerate(ps):
                        mm = nc.tensor.matmul(out[:, lo:hi], qs[:, q:q + P], ks[:, 0:k], start=(n == 0),
                                              stop=(n == len(ps) - 1))
                return mm
            return scores

        def rope_pe(pe, r0, pairs, rot, ready):
            for k, dst in enumerate(pairs):
                r = r0 + k
                ready(pe, k)
                if r >= 2:
                    pe.wait_ge(sem["rs_ready"], r - 1)
                n = dst.shape[1] * T
                nc.tensor.matmul(PB[4 + r % 2][:, 0:n], rot, dst.rearrange("p m t -> p (m t)"), start=True,
                                 stop=True).then_inc(sem["rot_mm"], 1)

        def rope_dve(dve, r0, pairs, temp):
            for k, dst in enumerate(pairs):
                r, m = r0 + k, dst.shape[1]
                dve.wait_ge(sem["rot_mm"], r + 1)
                if r >= 2:
                    dve.wait_ge(sem["rope_done"], r - 1)
                nc.vector.tensor_tensor(A[:, temp + 2 * (r % 2):temp + 2 * (r % 2) + m, :],
                                        PB[4 + r % 2][:, 0:m * T].rearrange("p (m t) -> p m t", m=m),
                                        SIN[:, :].unsqueeze(1).broadcast_to([P, m, T]), ALU.mult).then_inc(sem["rs_ready"], 1)

        def rope_pool(pool, own, r0, pairs, temp):
            for k, dst in enumerate(pairs):
                r, m = r0 + k, dst.shape[1]
                pool.wait_ge(sem["rot_mm"], r + 1)
                own(nc.gpsimd.tensor_tensor(dst, dst, COS[:, :].unsqueeze(1).broadcast_to([P, m, T]), ALU.mult))
                own.wait()
                pool.wait_ge(sem["rs_ready"], r + 1)
                nc.gpsimd.tensor_tensor(dst, dst, A[:, temp + 2 * (r % 2):temp + 2 * (r % 2) + m, :],
                                        ALU.add).then_inc(sem["rope_done"], 1)

        PI = math.pi
        C1 = 6.28125
        C2 = math.floor((2 * PI - C1) * 2 ** 20) / 2 ** 20
        C3 = 2 * PI - C1 - C2
        ROUND = 1.5 * 2 ** 23
        PINT, PF, T1, T2, T3 = (A[:, 40 + k, :] for k in range(5))

        def load_pool(pool, dst, src):
            pool.dma_start(dst, src).then_inc(sem["aux_in"], 16)

        def wait_load(eng, name):
            eng.wait_ge(sem["aux_in"], 16 * (LOADS.index(name) + 1))

        def tables_dve(dve, own, name, inv):
            wait_load(dve, name)
            own(nc.vector.tensor_copy(PF, PINT.bitcast(I32)))
            own.wait()
            own(nc.vector.tensor_scalar(PF, PF, inv, None, ALU.mult))
            own.wait()
            for j, shift in enumerate((0.0, 0.25)):
                t = T3 if j == 0 else T1
                own(nc.vector.tensor_scalar(T2, PF, 1.0 / (2 * PI), shift, ALU.mult, ALU.add))
                own.wait()
                own(nc.vector.tensor_scalar(T2, T2, ROUND, None, ALU.add))
                own.wait()
                own(nc.vector.tensor_scalar(T2, T2, -ROUND, None, ALU.add))
                own.wait()
                own(nc.vector.scalar_tensor_tensor(out=t, in0=T2, scalar=-C1, in1=PF, op0=ALU.mult, op1=ALU.add))
                own.wait()
                own(nc.vector.scalar_tensor_tensor(out=t, in0=T2, scalar=-C2, in1=t, op0=ALU.mult, op1=ALU.add))
                own.wait()
                own(nc.vector.scalar_tensor_tensor(out=t, in0=T2, scalar=-C3, in1=t, op0=ALU.mult, op1=ALU.add))
                own.wait()
                if j:
                    own(nc.vector.tensor_scalar(t, t, PI / 2, None, ALU.add))
                    own.wait()
                nc.vector.tensor_scalar(t, t, -3.1415925, 3.1415925, ALU.max, ALU.min).then_inc(sem["ang_ready"], 1)

        def tables_act(act, k):
            act.wait_ge(sem["ang_ready"], 2 * k + 2)
            nc.scalar.activation(SIN[:, :], T3, ACT.Sin).then_inc(sem["sincos"], 1)
            nc.scalar.activation(COS[:, :], T1, ACT.Sin).then_inc(sem["sincos"], 1)

        Z, XBC, XDT, XDE, BTOK, STATE, CBM, SEG, GW, ECS, CEX = 0, 16, 40, 48, 50, 52, 56, 60, 64, 68, 70
        WDT = A[:, 74, :].rearrange("p (k n) -> p k n", k=8)
        DTP = PB[4][:, 0:64].rearrange("p (c h) -> p c h", c=2)
        small = lambda k: SC[:, 64 + 64 * k:128 + 64 * k].rearrange("p (c h) -> p c h", c=2)
        DT, NA, DTA, CS = small(0), small(1), small(2), small(3)
        EAL = SC[:, 320:352]
        DTE = SC[:, 352:384]

        def over_chunks(a):
            return a.unsqueeze(1).broadcast_to([P, 2, 32])

        def conv_act(act, name, p, b, K, first, cw, cb, stride, col):
            for j in range(2):
                ins = nc.scalar.activation(first(j), bank(b)[:, j, :], ACT.Identity, bias=vec(cb, col + j),
                                           scale=vec(cw, (K - 1) * stride + col + j))
            ins.then_inc(sem["conv_base"], 1)

        def conv_dve(dve, own, n, b, K, dst, cw, cw0, stride, col):
            dve.wait_ge(sem["conv_base"], n + 1)
            for s in range(1, K):
                for j in range(2):
                    d = dst(j)
                    ins = nc.vector.scalar_tensor_tensor(
                        out=d[:, s:T], in0=bank(b)[:, j, 0:T - s], scalar=vec(cw, cw0 + (K - 1 - s) * stride + col + j),
                        in1=d[:, s:T], op0=ALU.mult, op1=ALU.add)
                    if s < K - 1:
                        own(ins)
                if s < K - 1:
                    own.wait()
            ins.then_inc(evac[b], 1)

        def ssm_in_pe(pe):
            pe.wait_ge(sem["vec_in"], 32)
            norm_pe(pe, "b1_0_in")
            pe.wait_ge(sem["normed"], 8)
            wait_load(pe, "wdt")
            for c in range(2):
                for k in range(DC):
                    mm = nc.tensor.matmul(DTP[:, c, :], H[:, k, c * P:c * P + P], WDT[:, k, :], start=(k == 0),
                                          stop=(k == DC - 1))
            mm.then_inc(sem["dt_mm"], 1)
            linear_pe(pe, "ssm_x", ht)
            linear_pe(pe, "ssm_z", ht)
            pe.wait_ge(sem["dta_ready"], 1)
            for c in range(2):
                nc.tensor.matmul(PB[5][:, c * 32:c * 32 + 32], upto, DTA[:, c, :], start=True, stop=True)
            nc.tensor.matmul(PB[5][:, 64:96], ones, DTA[:, 0, :], start=True, stop=True).then_inc(sem["cs_mm"], 1)

        def ssm_in_act(act, own):
            act.wait_ge(sem["vec_in"], 32)
            act.wait_ge(sem["x_in"], 16)
            norm_act(act, "b1_0_in", xt)
            nc.scalar.activation(EAL, vec("A_log", 0, 32), ACT.Exp)
            act.wait_ge(sem["dt_abs"], 1)
            own(nc.scalar.activation(NA, NA, ACT.Exp))
            own.wait()
            nc.scalar.activation(NA, NA, ACT.Ln, bias=1.0).then_inc(sem["dt_ln"], 1)
            for p in range(13):
                if p < 12:
                    b = wait_pair(act, "ssm_x", p)
                    conv_act(act, "ssm_x", p, b, 4, lambda j: A[:, XBC + 2 * p + j, :], "ssm_cw", "ssm_cb", 24, 2 * p)
                if p >= 1:
                    wait_evac(act, "ssm_x", p - 1)
                    xb = A[:, XBC + 2 * p - 2:XBC + 2 * p, :]
                    nc.scalar.activation(xb, xb, ACT.Silu).then_inc(sem["xbc_ready"], 1)
            copy_out_act(act, "ssm_z", Z, ACT.Silu)
            act.wait_ge(sem["dte_in"], 1)
            nc.scalar.activation(DTE, DTE, ACT.Exp).then_inc(sem["dte_ready"], 1)

        def ssm_in_dve(dve, own):
            dve.wait_ge(sem["vec_in"], 32)
            norm_dve(dve, "b1_0_in", xt, lambda t: vec("norm_g", t), ht)
            dve.wait_ge(sem["dt_mm"], 1)
            own(nc.vector.tensor_tensor(DT, DTP, over_chunks(vec("dt_b", 0, 32)), ALU.add))
            own.wait()
            for c in range(2):
                ins = nc.vector.scalar_tensor_tensor(out=NA[:, c], in0=DT[:, c], scalar=-1.0, in1=DT[:, c],
                                                     op0=ALU.mult, op1=ALU.min)
            ins.then_inc(sem["dt_abs"], 1)
            dve.wait_ge(sem["dt_ln"], 1)
            for c in range(2):
                ins = nc.vector.scalar_tensor_tensor(out=DT[:, c], in0=DT[:, c], scalar=0.0, in1=NA[:, c], op0=ALU.max,
                                                     op1=ALU.add)
            ins.then_inc(sem["dt_ready"], 1)
            dve.wait_ge(sem["dt_ready"], 1)
            for c in range(2):
                ins = nc.vector.scalar_tensor_tensor(out=DTA[:, c], in0=DT[:, c], scalar=-1.0, in1=EAL, op0=ALU.mult,
                                                     op1=ALU.mult)
            ins.then_inc(sem["dta_ready"], 1)
            for p in range(12):
                conv_dve(dve, own, p, pair_of("ssm_x", p) % NB, 4, lambda j: A[:, XBC + 2 * p + j, :], "ssm_cw", 0, 24,
                         2 * p)
            dve.wait_ge(sem["cs_mm"], 1)
            own(nc.vector.tensor_copy(CS, PB[5][:, 0:64].rearrange("p (c h) -> p c h", c=2)))
            own.wait()
            nc.vector.tensor_tensor(DTE, PB[5][:, 64:96], CS[:, 0, :], ALU.subtract).then_inc(sem["dte_in"], 1)

        def ssm_in_pool(pool, own):
            load_pool(pool, WDT, io["wdt"])

        def batch(i):
            return i // 4, i // 2 % 2, i % 2

        def xdt(g, c):
            return flat(XDT + 4 * (g % 2) + 2 * c, 2)

        def ssm_core_pe(pe):
            for c in range(2):
                for g in range(4):
                    mm = nc.tensor.matmul(PB[c][:, g * P:g * P + P], A[:, XBC + 16 + g, c * P:c * P + P],
                                          A[:, XBC + 20 + g, c * P:c * P + P], start=True, stop=True)
                mm.then_inc(sem["cb_mm"], 1)
            for g in range(4):
                mm = nc.tensor.transpose(PB[7][:, g * P:g * P + P], A[:, XBC + 16 + g, 0:P], ident)
            mm.then_inc(sem["bt_mm"], 1)
            for i in range(17):
                if i < 16:
                    g, half, c = batch(i)
                    if i % 4 == 0:
                        if g:
                            pe.wait_ge(sem["xdt_ready"], 2 * g)
                        for cc in range(2):
                            for k in range(4):
                                mm = nc.tensor.transpose(PB[2 + cc][:, k * P:k * P + P],
                                                         A[:, XBC + 4 * g + k, cc * P:cc * P + P], ident)
                            mm.then_inc(sem["xt_mm"], 1)
                    if i >= 2:
                        pe.wait_ge(sem["seg_ready"], i - 1)
                    if i >= 3:
                        pe.wait_ge(sem["ecs_ready"], (i - 1) // 2)
                    for k in range(4):
                        h = g * HPG + half * 4 + k
                        mm = nc.tensor.matmul(PB[4 + i % 2][:, k * P:k * P + P], DTA[:, c, h:h + 1].broadcast_to([P, P]),
                                              upto, start=True, stop=True)
                    mm.then_inc(sem["cr_mm"], 1)
                    if i % 4 == 0:
                        pe.wait_ge(sem["btok_ready"], 1)
                        pe.wait_ge(sem["xde_ready"], g + 1)
                        if g:
                            pe.wait_ge(sem["st_ready"], g)
                        nc.tensor.matmul(PB[6][:, :], flat(BTOK, 2)[:, g * P:g * P + P], flat(XDE, 2), start=True,
                                         stop=True).then_inc(sem["st_mm"], 1)
                if i >= 1:
                    j = i - 1
                    g, half, c = batch(j)
                    pe.wait_ge(sem["g_ready"], j + 1)
                    if j >= 2:
                        pe.wait_ge(sem["y_ready"], j - 1)
                    else:
                        pe.wait_ge(sem["cbm_ready"], 2)
                    if c:
                        pe.wait_ge(sem["cp_ready"], j // 2 + 1)
                        pe.wait_ge(sem["st_ready"], g + 1)
                    for k in range(4):
                        o = PB[j % 2][64 * (k % 2):64 * (k % 2) + 64, k // 2 * P:k // 2 * P + P]
                        hs = slice((half * 4 + k) * 64, (half * 4 + k) * 64 + 64)
                        mm = nc.tensor.matmul(o, xdt(g, c)[:, hs], flat(GW + 2 * (j % 2), 2)[:, k * P:k * P + P],
                                              start=True, stop=(c == 0))
                        if c:
                            mm = nc.tensor.matmul(o, flat(STATE + 2 * (g % 2), 2)[:, hs],
                                                  flat(CEX + 2 * (half % 2), 2)[:, k * P:k * P + P], start=False, stop=True)
                    mm.then_inc(sem["y_mm"], 1)

        def ssm_core_act(act, own):
            act.wait_ge(sem["bt_mm"], 1)
            nc.scalar.activation(flat(BTOK, 2), PB[7][:, :], ACT.Identity).then_inc(sem["btok_ready"], 1)
            for i in range(16):
                g, half, c = batch(i)
                act.wait_ge(sem["seg_ready"], i + 1)
                if c:
                    if i >= 3:
                        act.wait_ge(sem["cp_ready"], i // 2)
                    nc.scalar.activation(flat(ECS, 2), PB[4 + i % 2][:, :], ACT.Exp).then_inc(sem["ecs_ready"], 1)
                s = flat(SEG + 2 * (i % 2), 2)
                nc.scalar.activation(s, s, ACT.Exp).then_inc(sem["e_ready"], 1)
                if i % 4 == 0:
                    act.wait_ge(sem["st_mm"], g + 1)
                    if g >= 2:
                        act.wait_ge(sem["y_mm"], 4 * (g - 1))
                    nc.scalar.activation(flat(STATE + 2 * (g % 2), 2), PB[6][:, :], ACT.Identity).then_inc(sem["st_ready"], 1)

        def ssm_core_dve(dve, own):
            for c in range(2):
                dve.wait_ge(sem["cb_mm"], c + 1)
                nc.vector.tensor_tensor(flat(CBM + 2 * c, 2).rearrange("p (g t) -> p g t", g=4),
                                        PB[c][:, :].rearrange("p (g t) -> p g t", g=4),
                                        upto.unsqueeze(1).broadcast_to([P, 4, P]), ALU.mult).then_inc(sem["cbm_ready"], 1)
            dve.wait_ge(sem["cbm_ready"], 2)
            for i in range(18):
                if i < 16:
                    g, half, c = batch(i)
                    if i % 4 == 0:
                        if g >= 2:
                            dve.wait_ge(sem["y_mm"], 4 * (g - 1))
                        for cc in range(2):
                            dve.wait_ge(sem["xt_mm"], 2 * g + cc + 1)
                            nc.vector.tensor_tensor(
                                xdt(g, cc).rearrange("p (h d) -> p h d", h=HPG),
                                PB[2 + cc][:, :].rearrange("p (h d) -> p h d", h=HPG),
                                DT[:, cc, g * HPG:g * HPG + HPG].unsqueeze(2).broadcast_to([P, HPG, SSM_P]),
                                ALU.mult).then_inc(sem["xdt_ready"], 1)
                    dve.wait_ge(sem["cr_mm"], i + 1)
                    for k in range(4):
                        h = g * HPG + half * 4 + k
                        ins = nc.vector.tensor_scalar(flat(SEG + 2 * (i % 2), 2)[:, k * P:k * P + P],
                                                      PB[4 + i % 2][:, k * P:k * P + P], CS[:, c, h:h + 1], 0.0,
                                                      ALU.subtract, ALU.min)
                    ins.then_inc(sem["seg_ready"], 1)
                if 1 <= i <= 16:
                    j = i - 1
                    g, half, c = batch(j)
                    dve.wait_ge(sem["e_ready"], j + 1)
                    if j >= 2:
                        dve.wait_ge(sem["y_mm"], j - 1)
                    nc.vector.tensor_tensor(
                        flat(GW + 2 * (j % 2), 2).rearrange("p (k t) -> p k t", k=4),
                        flat(SEG + 2 * (j % 2), 2).rearrange("p (k t) -> p k t", k=4),
                        flat(CBM + 2 * c, 2)[:, g * P:g * P + P].unsqueeze(1).broadcast_to([P, 4, P]),
                        ALU.mult).then_inc(sem["g_ready"], 1)
                if i >= 2:
                    j = i - 2
                    g, half, c = batch(j)
                    dve.wait_ge(sem["y_mm"], j + 1)
                    for m in range(2):
                        t = 4 * g + half * 2 + m
                        y = A[:, XBC + t, c * P:c * P + P]
                        ins = nc.vector.scalar_tensor_tensor(out=y, in0=y, scalar=vec("ssm_D", t),
                                                             in1=PB[j % 2][:, m * P:m * P + P], op0=ALU.mult, op1=ALU.add)
                    ins.then_inc(sem["y_ready"], 1)

        def ssm_core_pool(pool, own):
            for g in range(4):
                pool.wait_ge(sem["xdt_ready"], 2 * g + 1)
                pool.wait_ge(sem["dte_ready"], 1)
                if g:
                    pool.wait_ge(sem["st_mm"], g)
                nc.gpsimd.tensor_tensor(flat(XDE, 2).rearrange("p (h d) -> p h d", h=HPG),
                                        xdt(g, 0).rearrange("p (h d) -> p h d", h=HPG),
                                        DTE[:, g * HPG:g * HPG + HPG].unsqueeze(2).broadcast_to([P, HPG, SSM_P]),
                                        ALU.mult).then_inc(sem["xde_ready"], 1)
                for half in range(2):
                    n = 2 * g + half
                    pool.wait_ge(sem["ecs_ready"], n + 1)
                    if n >= 2:
                        pool.wait_ge(sem["y_mm"], 2 * n - 2)
                    nc.gpsimd.tensor_tensor(flat(CEX + 2 * (half % 2), 2).rearrange("p (k t) -> p k t", k=4),
                                            flat(ECS, 2).rearrange("p (k t) -> p k t", k=4),
                                            A[:, XBC + 20 + g, P:T].unsqueeze(1).broadcast_to([P, 4, P]),
                                            ALU.mult).then_inc(sem["cp_ready"], 1)

        yt = tiles(XBC)

        def ssm_out_pe(pe):
            norm_pe(pe, "ssm")
            linear_pe(pe, "ssm_out", yt, ready=normed_ready("ssm"))
            norm_pe(pe, "b1_0_mix")

        def ssm_out_act(act, own):
            def gated(eng, t):
                q = t // 2
                eng.wait_ge(sem["gy_pool"] if q % 2 else sem["gy_dve"], q // 2 + 1)
            norm_act(act, "ssm", yt, gated)
            copy_out_act(act, "ssm_out", MIX)
            norm_act(act, "b1_0_mix", mix, lambda e, t: wait_evac(e, "ssm_out", t // 2))

        def gate(eng, q):
            y, z = (A[:, b + 2 * q:b + 2 * q + 2, :] for b in (XBC, Z))
            return eng.tensor_tensor(y, y, z, ALU.mult)

        def ssm_out_dve(dve, own):
            for q in range(0, 8, 2):
                gate(nc.vector, q).then_inc(sem["gy_dve"], 1)
            norm_dve(dve, "ssm", yt, lambda t: vec("ssm_ng", t), yt)
            norm_dve(dve, "b1_0_mix", mix, lambda t: vec("norm_g", 8 + t), mix)

        def ssm_out_pool(pool, own):
            for q in range(1, 8, 2):
                gate(nc.gpsimd, q).then_inc(sem["gy_pool"], 1)
            residual_pool(pool, "b1_0_mix", 0)

        MEM, XK, XV, XQ, XO = 0, 8, 16, 24, 32
        memt = tiles(MEM)
        XA_A0 = {0: 0, 1: 4}

        def xattn_pe(pe, l):
            norm_pe(pe, f"mem{l}")
            norm_pe(pe, f"xa_in{l}")
            linear_pe(pe, f"xa_k{l}", memt, ready=normed_ready(f"mem{l}"))
            linear_pe(pe, f"xa_v{l}", memt, tokens=True)
            linear_pe(pe, f"xa_q{l}", ht, ready=normed_ready(f"xa_in{l}"))
            for p in range(4):
                wait_evac(pe, f"xa_q{l}", p)

            def scores(h, c, out):
                for m in range(2):
                    for d in range(2):
                        mm = nc.tensor.matmul(out[:, m * T:m * T + T], A[:, XQ + 2 * h + d, m * P:m * P + P],
                                              A[:, XK + 2 * h + d, :], start=(d == 0), stop=(d == 1))
                return mm

            def pv(h, pt, out):
                v = flat(XV, 8).rearrange("p (m n) -> p m n", m=2)
                for d in range(2):
                    for m in range(2):
                        mm = nc.tensor.matmul(out[:, d * T:d * T + T], v[:, m, (2 * h + d) * P:(2 * h + d) * P + P],
                                              pt[:, m * T:m * T + T], start=(m == 0), stop=(m == 1))
                return mm
            attend_pe(pe, 4, XA_A0[l], XA_A0[l], 1, False, scores, pv)
            pe.wait_ge(sem["o_evac"], XA_A0[l] + 4)
            linear_pe(pe, f"xa_o{l}", tiles(XO))
            norm_pe(pe, f"xa_out{l}")

        def xattn_act(act, own, l):
            wait_load(act, f"mem{l}")
            norm_act(act, f"mem{l}", memt)
            norm_act(act, f"xa_in{l}", xt)
            copy_out_act(act, f"xa_k{l}", XK)
            copy_out_act(act, f"xa_v{l}", XV, tokens=D)
            copy_out_act(act, f"xa_q{l}", XQ)
            attend_act(act, 4, XA_A0[l], XA_A0[l], 1, False,
                       lambda h, o: (flat(XO + 2 * h, 2), o[:, :]))
            copy_out_act(act, f"xa_o{l}", MIX)
            norm_act(act, f"xa_out{l}", mix, lambda e, t: wait_evac(e, f"xa_o{l}", t // 2))

        def xattn_dve(dve, own, l):
            norm_dve(dve, f"mem{l}", memt, lambda t: vec("mem_g", 8 * l + t), memt)
            norm_dve(dve, f"xa_in{l}", xt, lambda t: vec("norm_g", (6 * l + 2) * 8 + t), ht)
            attend_dve(dve, own, 4, XA_A0[l], XA_A0[l], 1, False, 1.0 / 16)
            norm_dve(dve, f"xa_out{l}", mix, lambda t: vec("norm_g", (6 * l + 3) * 8 + t), mix)

        def xattn_pool(pool, own, l):
            load_pool(pool, A[:, MEM:MEM + 8, :], io["mem"])
            residual_pool(pool, f"xa_out{l}", 3 * l + 1)

        FF, UG, UV = 0, 22, 26
        CB0 = {0: 12, 1: 34}

        def branch(base, q):
            return lambda j: A[:, base + 2 * (q % 2) + j, :]

        def ffn_pe(pe, l):
            norm_pe(pe, f"ff_in{l}")
            linear_pe(pe, f"ffn_in{l}", ht, ready=normed_ready(f"ff_in{l}"))
            linear_pe(pe, f"ffn_out{l}", tiles(FF),
                      ready=lambda e, kc: e.wait_ge(sem["ff_ready"], 11 * l + kc // 2 + 1))
            norm_pe(pe, f"ff_out{l}")

        def ffn_act(act, own, l):
            norm_act(act, f"ff_in{l}", xt)
            for p in range(23):
                if p < 22:
                    q = p // 2
                    b = wait_pair(act, f"ffn_in{l}", p)
                    if q >= 2:
                        act.wait_ge(sem["ff_ready"], 11 * l + q - 1)
                    col = (22 if p % 2 else 0) + 2 * q
                    for j in range(2):
                        ins = nc.scalar.activation(branch(UV if p % 2 else UG, q)(j), bank(b)[:, j, :], ACT.Identity,
                                                   bias=vec("ffn_cb", 44 * l + col + j),
                                                   scale=vec("ffn_cw", (3 * l + 2) * 44 + col + j))
                    ins.then_inc(sem["conv_base"], 1)
                if p % 2 == 1:
                    q = p // 2
                    wait_evac(act, f"ffn_in{l}", p - 1)
                    u = A[:, UG + 2 * (q % 2):UG + 2 * (q % 2) + 2, :]
                    nc.scalar.activation(u, u, ACT.Silu).then_inc(sem["sg_ready"], 1)
            copy_out_act(act, f"ffn_out{l}", MIX)
            norm_act(act, f"ff_out{l}", mix, lambda e, t: wait_evac(e, f"ffn_out{l}", t // 2))

        def ffn_dve(dve, own, l):
            norm_dve(dve, f"ff_in{l}", xt, lambda t: vec("norm_g", (6 * l + 4) * 8 + t), ht)
            for p in range(22):
                q = p // 2
                conv_dve(dve, own, CB0[l] + p, pair_of(f"ffn_in{l}", p) % NB, 3, branch(UV if p % 2 else UG, q),
                         "ffn_cw", 3 * l * 44, 44, (22 if p % 2 else 0) + 2 * q)
            norm_dve(dve, f"ff_out{l}", mix, lambda t: vec("norm_g", (6 * l + 5) * 8 + t), mix)

        def ffn_pool(pool, own, l):
            for q in range(11):
                pool.wait_ge(sem["sg_ready"], 11 * l + q + 1)
                wait_evac(pool, f"ffn_in{l}", 2 * q + 1)
                nc.gpsimd.tensor_tensor(A[:, FF + 2 * q:FF + 2 * q + 2, :], A[:, UG + 2 * (q % 2):UG + 2 * (q % 2) + 2, :],
                                        A[:, UV + 2 * (q % 2):UV + 2 * (q % 2) + 2, :], ALU.mult).then_inc(sem["ff_ready"], 1)
            residual_pool(pool, f"ff_out{l}", 3 * l + 2)

        CIN, CV, SIG = 0, 8, 16
        cvt = tiles(CV)
        MEAN = A[:, 20, :]

        def conf_pe(pe):
            norm_pe(pe, "b1_1_in")
            linear_pe(pe, "pw1", ht, ready=normed_ready("b1_1_in"))
            for t in range(8):
                pe.wait_ge(sem["cv_ready"], t // 2 + 1)
                mm = nc.tensor.matmul(PB[6][:, 0:T], ones, cvt(t), start=(t == 0), stop=(t == 7))
            mm.then_inc(sem["mean_mm"], 1)
            norm_pe(pe, "ln")
            linear_pe(pe, "pw2", cvt, ready=lambda e, kc: e.wait_ge(sem["ln_out"], kc + 1))
            norm_pe(pe, "b1_1_mix")

        def conf_act(act, own):
            norm_act(act, "b1_1_in", xt)
            for q in range(4):
                b = wait_pair(act, "pw1", 2 * q)
                if q >= 2:
                    wait_evac(act, "pw1", 2 * q - 3)
                for j in range(2):
                    ins = nc.scalar.activation(A[:, SIG + 2 * (q % 2) + j, :], bank(b)[:, j, :], ACT.Sigmoid,
                                               bias=vec("pw1_b", 8 + 2 * q + j))
                ins.then_inc(evac[b], 1)
                wait_evac(act, "pw1", 2 * q + 1)
                for j in range(2):
                    ins = nc.scalar.activation(cvt(2 * q + j), A[:, CIN + 2 * q + j, :], ACT.Identity,
                                               bias=vec("dw_b", 2 * q + j), scale=vec("dw_w", (CF_K - 1) * 8 + 2 * q + j))
                ins.then_inc(sem["cv_base"], 1)
            norm_act(act, "ln", cvt, lambda e, t: e.wait_ge(sem["centered"], t // 4 + 1))
            for t in range(8):
                act.wait_ge(sem["normed"], NORM["ln"][2] + t + 1)
                nc.scalar.activation(cvt(t), cvt(t), ACT.Silu, bias=vec("ln_b", t)).then_inc(sem["ln_out"], 1)
            for p in range(4):
                b = wait_pair(act, "pw2", p)
                for j in range(2):
                    ins = nc.scalar.activation(mix(2 * p + j), bank(b)[:, j, :], ACT.Identity, bias=vec("pw2_b", 2 * p + j))
                ins.then_inc(evac[b], 1)
            norm_act(act, "b1_1_mix", mix, lambda e, t: wait_evac(e, "pw2", t // 2))

        def conf_dve(dve, own):
            norm_dve(dve, "b1_1_in", xt, lambda t: vec("norm_g", 48 + t), ht)
            for q in range(4):
                b = wait_pair(dve, "pw1", 2 * q + 1)
                wait_evac(dve, "pw1", 2 * q)
                for j in range(2):
                    ins = nc.vector.scalar_tensor_tensor(out=A[:, CIN + 2 * q + j, :], in0=bank(b)[:, j, :],
                                                         scalar=vec("pw1_b", 2 * q + j),
                                                         in1=A[:, SIG + 2 * (q % 2) + j, :], op0=ALU.add, op1=ALU.mult)
                ins.then_inc(evac[b], 1)
                wait_evac(dve, "pw1", 2 * q + 1)
                dve.wait_ge(sem["cv_base"], q + 1)
                for s in range(1, CF_K):
                    for j in range(2):
                        t = 2 * q + j
                        ins = nc.vector.scalar_tensor_tensor(
                            out=cvt(t)[:, s:T], in0=A[:, CIN + t, 0:T - s], scalar=vec("dw_w", (CF_K - 1 - s) * 8 + t),
                            in1=cvt(t)[:, s:T], op0=ALU.mult, op1=ALU.add)
                        if s < CF_K - 1:
                            own(ins)
                    if s < CF_K - 1:
                        own.wait()
                ins.then_inc(sem["cv_ready"], 1)
            dve.wait_ge(sem["mean_mm"], 1)
            own(nc.vector.tensor_scalar(MEAN, PB[6][:, 0:T], 1.0 / D, None, ALU.mult))
            own.wait()
            for k in range(2):
                c = A[:, CV + 4 * k:CV + 4 * k + 4, :]
                nc.vector.tensor_tensor(c, c, MEAN.unsqueeze(1).broadcast_to([P, 4, T]),
                                        ALU.subtract).then_inc(sem["centered"], 1)
            norm_dve(dve, "ln", cvt, lambda t: vec("ln_g", t), cvt)
            norm_dve(dve, "b1_1_mix", mix, lambda t: vec("norm_g", 56 + t), mix)

        def conf_pool(pool, own):
            residual_pool(pool, "b1_1_mix", 3)

        def add_out_dve(dve, name):
            for p in range(LIN[name][1]):
                b = wait_pair(dve, name, p)
                x = X[:, 2 * p:2 * p + 2, :]
                nc.vector.tensor_tensor(x, x, bank(b), ALU.add).then_inc(evac[b], 1)

        AQ, AK, AV, BQ, BK, BV, EO, ROPE = 0, 4, 8, 12, 16, 20, 24, 32
        STRICT = flat(48, 3)[:, 0:384]
        NOTYET = flat(48, 3)[:, 384:768]
        LAMP, LAME, LAM, SUBG = SC[:, 24:32], SC[:, 32:40], SC[:, 40:44], SC[:, 44:45]
        LAM_INIT = 0.8 - 0.6 * math.exp(0.0)
        A0 = {"diff": 8, "moba": 16, "mla": 32}
        B0 = {"diff": 8, "moba": 12, "mla": 28}
        SBH = 8

        def stick(i, k):
            at = ((i % 3) * 4 + k) * 384
            return flat(52, 18)[:, at:at + 384]

        def pair_tiles(base, n):
            return [A[:, base + 2 * k:base + 2 * k + 2, :] for k in range(n)]

        def stick_pe(pe):
            for i in range(SBH + 3):
                if i < SBH:
                    if i >= 2:
                        pe.wait_ge(sem["zabs_ready"], i - 1)
                    rows = slice(64 * (i % 2), 64 * (i % 2) + 64)
                    q, k = A[rows, AQ + i // 2, :], A[rows, AK + i // 2, :]
                    nc.tensor.matmul(PB[4 + i % 2][:, 0:T], k[:, 0:P], q, start=True, stop=True)
                    nc.tensor.matmul(PB[4 + i % 2][:, T:384], k[:, P:T], q[:, P:T], start=True,
                                     stop=True).then_inc(sem["z_mm"], 1)
                if 1 <= i <= SBH:
                    j = i - 1
                    s = stick(j, 2)
                    pe.wait_ge(sem["spm_ready"], j + 1)
                    if j >= 2:
                        pe.wait_ge(sem["rs_read"], j - 1)
                    o = PB[6 + j % 2]
                    nc.tensor.matmul(o[:, 0:T], onward, s[:, 0:T], start=True, stop=False)
                    nc.tensor.matmul(o[:, P:T], ones, s[:, T:384], start=False, stop=True)
                    nc.tensor.matmul(o[:, T:384], onward, s[:, T:384], start=True, stop=True).then_inc(sem["rs_mm"], 1)
                if i >= 3:
                    j = i - 3
                    pe.wait_ge(sem["sw_ready"], j + 1)
                    if j >= 2:
                        pe.wait_ge(sem["so_evac"], j - 1)
                    v = flat(AV, 4).rearrange("p (m n) -> p m n", m=2)
                    o = PB[2 + j % 2][64 * (j % 2):64 * (j % 2) + 64, 0:T]
                    w = stick(j, 3)
                    nc.tensor.matmul(o, v[:, 0, 64 * j:64 * j + 64], w[:, 0:T], start=True, stop=False)
                    nc.tensor.matmul(o[:, P:T], v[:, 1, 64 * j:64 * j + 64], w[:, T:384], start=False,
                                     stop=True).then_inc(sem["so_mm"], 1)

        def stick_act(act, own):
            for i in range(SBH + 4):
                if i < SBH:
                    n = stick(i, 1)
                    act.wait_ge(sem["zabs_ready"], i + 1)
                    own(nc.scalar.activation(n, n, ACT.Exp))
                    own.wait()
                    nc.scalar.activation(n, n, ACT.Ln, bias=1.0).then_inc(sem["zln_ready"], 1)
                if 2 <= i < SBH + 2:
                    w = stick(i - 2, 3)
                    act.wait_ge(sem["rs_read"], i - 1)
                    nc.scalar.activation(w, w, ACT.Exp).then_inc(sem["sw_ready"], 1)
                if 3 <= i < SBH + 3:
                    j = i - 3
                    act.wait_ge(sem["so_mm"], j + 1)
                    rows = slice(64 * (j % 2), 64 * (j % 2) + 64)
                    nc.scalar.activation(A[rows, EO + j // 2, :], PB[2 + j % 2][rows, 0:T],
                                         ACT.Identity).then_inc(sem["so_evac"], 1)

        def stick_dve(dve, own):
            for i in range(SBH + 2):
                if i < SBH:
                    dve.wait_ge(sem["z_mm"], i + 1)
                    own(nc.vector.tensor_scalar(stick(i, 0), PB[4 + i % 2][:, 0:384], 0.125, None, ALU.mult))
                    own.wait()
                    nc.vector.scalar_tensor_tensor(out=stick(i, 1), in0=stick(i, 0), scalar=-1.0, in1=stick(i, 0),
                                                   op0=ALU.mult, op1=ALU.min).then_inc(sem["zabs_ready"], 1)
                if 1 <= i <= SBH:
                    j = i - 1
                    dve.wait_ge(sem["zln_ready"], j + 1)
                    if j >= 3:
                        dve.wait_ge(sem["rs_mm"], j - 2)
                    own(nc.vector.scalar_tensor_tensor(out=stick(j, 2), in0=stick(j, 0), scalar=0.0, in1=stick(j, 1),
                                                       op0=ALU.max, op1=ALU.add))
                    own.wait()
                    nc.vector.tensor_tensor(stick(j, 2), stick(j, 2), STRICT, ALU.mult).then_inc(sem["spm_ready"], 1)
                if i >= 2:
                    j = i - 2
                    dve.wait_ge(sem["rs_mm"], j + 1)
                    if j >= 3:
                        dve.wait_ge(sem["so_mm"], j - 2)
                    own(nc.vector.scalar_tensor_tensor(out=stick(j, 3), in0=PB[6 + j % 2][:, 0:384], scalar=-1.0,
                                                       in1=stick(j, 0), op0=ALU.mult, op1=ALU.add))
                    own.wait()
                    nc.vector.scalar_tensor_tensor(out=stick(j, 3), in0=stick(j, 3), scalar=0.0, in1=NOTYET,
                                                   op0=ALU.min, op1=ALU.add).then_inc(sem["rs_read"], 1)

        def headnorm_pe(pe, n0, pairs):
            for q in range(pairs):
                n = n0 + q
                pe.wait_ge(sem["hn_sq"], n + 1)
                if q >= 2:
                    pe.wait_ge(sem["hn_var"], n - 1)
                nc.tensor.matmul(PB[6 + n % 2][:, :], ones, flat(SQ + 2 * q, 2), start=True,
                                 stop=True).then_inc(sem["hn_stat"], 1)

        def headnorm_act(act, n0, src, ready):
            for q, s in enumerate(src):
                ready(act, q)
                nc.scalar.activation(flat(SQ + 2 * q, 2), s.rearrange("p m t -> p (m t)"),
                                     ACT.Square).then_inc(sem["hn_sq"], 1)
            for q in range(len(src)):
                v = flat(SQ + 8 + 2 * q, 2)
                act.wait_ge(sem["hn_var"], n0 + q + 1)
                nc.scalar.activation(v, v, ACT.Sqrt).then_inc(sem["hn_std"], 1)

        def headnorm_dve(dve, own, n0, src, gain, after=None):
            for q in range(len(src)):
                dve.wait_ge(sem["hn_stat"], n0 + q + 1)
                nc.vector.tensor_scalar(flat(SQ + 8 + 2 * q, 2), PB[6 + (n0 + q) % 2][:, :], 1.0 / P, EPS, ALU.mult,
                                        ALU.add).then_inc(sem["hn_var"], 1)
            for q, s in enumerate(src):
                v, s = flat(SQ + 8 + 2 * q, 2), s.rearrange("p m t -> p (m t)")
                dve.wait_ge(sem["hn_std"], n0 + q + 1)
                own(nc.vector.reciprocal(v, v))
                own.wait()
                ins = nc.vector.scalar_tensor_tensor(out=s, in0=s, scalar=gain, in1=v, op0=ALU.mult, op1=ALU.mult)
                if after:
                    own(ins)
                    own.wait()
                    ins = nc.vector.tensor_tensor(s, s, after(q), ALU.mult)
                ins.then_inc(sem["hn_out"], 1)

        even_rope = pair_tiles(BQ, 2) + pair_tiles(BK, 2)
        diff_out = pair_tiles(EO + 4, 2)

        def even_ready(eng, k):
            wait_evac(eng, "ab_bq" if k < 2 else "ab_bk", k % 2)

        def even_pe(pe):
            norm_pe(pe, "b2_0_in")
            pe.wait_ge(sem["lam_in"], 1)
            nc.tensor.matmul(PB[6][:, 0:8], ones, LAMP, start=True, stop=True).then_inc(sem["lam_mm"], 1)
            linear_pe(pe, "ab_aq", ht, ready=normed_ready("b2_0_in"))
            linear_pe(pe, "ab_ak", ht)
            linear_pe(pe, "ab_av", ht, tokens=True)
            linear_pe(pe, "ab_bq", ht)
            linear_pe(pe, "ab_bk", ht)
            linear_pe(pe, "ab_bv", ht, tokens=True)
            rope_pe(pe, 0, even_rope, rot2, even_ready)
            pe.wait_ge(sem["lam_ready"], 1)
            wait_evac(pe, "ab_bv", 0)
            wait_evac(pe, "ab_bv", 1)
            pe.wait_ge(sem["rs_ready"], 4)
            stick_pe(pe)
            pe.wait_ge(sem["rope_done"], 4)
            pe.wait_ge(sem["so_evac"], SBH)

            def parts(h, c):
                rows = slice(64 * c, 64 * c + 64)
                return [(A[rows, BQ + h, :], A[rows, BK + h, :])]
            v = flat(BV, 4).rearrange("p (m n) -> p m n", m=2)
            attend_pe(pe, 4, A0["diff"], B0["diff"], 2, True, scores_causal(parts),
                      pv_causal(lambda h, m: v[:, m, h * P:h * P + P], lambda h: slice(0, P)))
            headnorm_pe(pe, 0, 2)
            pe.wait_ge(sem["hn_out"], 2)
            linear_pe(pe, "ab_out", tiles(EO))

        def even_act(act, own):
            norm_act(act, "b2_0_in", xt)
            tables_act(act, 0)
            act.wait_ge(sem["lam_mm"], 1)
            nc.scalar.activation(LAME, PB[6][:, 0:8], ACT.Exp).then_inc(sem["lam_exp"], 1)
            copy_out_act(act, "ab_aq", AQ)
            copy_out_act(act, "ab_ak", AK)
            copy_out_act(act, "ab_av", AV, tokens=512)
            copy_out_act(act, "ab_bq", BQ)
            copy_out_act(act, "ab_bk", BK)
            copy_out_act(act, "ab_bv", BV, tokens=512)
            stick_act(act, own)
            attend_act(act, 4, A0["diff"], B0["diff"], 2, True, lambda h, o: (A[:, EO + 4 + h, :], o[:, 0:T]))
            headnorm_act(act, 0, diff_out, lambda e, q: e.wait_ge(sem["o_evac"], B0["diff"] + 2 * q + 2))

        def even_dve(dve, own):
            norm_dve(dve, "b2_0_in", xt, lambda t: vec("attn2", t), ht)
            for k in range(2):
                ins = nc.vector.tensor_tensor(LAMP[:, 4 * k:4 * k + 4], vec("lam", 8 * k, 4), vec("lam", 8 * k + 4, 4),
                                              ALU.mult)
            ins.then_inc(sem["lam_in"], 1)
            tables_dve(dve, own, "strict", vec("inv2", 0))
            dve.wait_ge(sem["lam_exp"], 1)
            own(nc.vector.tensor_tensor(LAM, LAME[:, 0:4], LAME[:, 4:8], ALU.subtract))
            own.wait()
            own(nc.vector.tensor_scalar(LAM, LAM, LAM_INIT, None, ALU.add))
            nc.vector.tensor_scalar(SUBG, vec("subln", 0), 1.0 - LAM_INIT, None, ALU.mult).then_inc(sem["lam_ready"], 1)
            dve.wait_ge(sem["sincos"], 2)
            own.wait()
            dve.wait_ge(sem["lam_ready"], 1)
            rope_dve(dve, 0, even_rope, ROPE)
            stick_dve(dve, own)
            attend_dve(dve, own, 4, A0["diff"], B0["diff"], 2, True, 0.125, lam=lambda h: LAM[:, h:h + 1])
            headnorm_dve(dve, own, 0, diff_out, SUBG)
            add_out_dve(dve, "ab_out")

        def even_pool(pool, own):
            load_pool(pool, A[:, 40, :].bitcast(I32), io["pos2"])
            load_pool(pool, flat(48, 3), io["strict"])
            pool.wait_ge(sem["sincos"], 2)
            rope_pool(pool, own, 0, even_rope, ROPE)

        moba_rope = pair_tiles(0, 4) + pair_tiles(8, 4)

        def moba_pe(pe):
            norm_pe(pe, "b2_1_in")
            linear_pe(pe, "mb_q", ht, ready=normed_ready("b2_1_in"))
            linear_pe(pe, "mb_k", ht)
            linear_pe(pe, "mb_v", ht, tokens=True)
            rope_pe(pe, 4, moba_rope, rot2, lambda e, k: wait_evac(e, "mb_q" if k < 4 else "mb_k", k % 4))
            for p in range(4):
                wait_evac(pe, "mb_v", p)
            pe.wait_ge(sem["rope_done"], 12)

            def parts(h, c):
                rows = slice(64 * (h % 2), 64 * (h % 2) + 64)
                return [(A[rows, h // 2, :], A[rows, 8 + h // 2, :])]
            v = flat(16, 8).rearrange("p (m n) -> p m n", m=2)
            attend_pe(pe, 16, A0["moba"], B0["moba"], 1, True, scores_causal(parts),
                      pv_causal(lambda h, m: v[:, m, h * 64:h * 64 + 64],
                                lambda h: slice(64 * (h % 2), 64 * (h % 2) + 64)))
            pe.wait_ge(sem["o_evac"], B0["moba"] + 16)
            linear_pe(pe, "mb_out", tiles(24))

        def moba_act(act, own):
            norm_act(act, "b2_1_in", xt)
            copy_out_act(act, "mb_q", 0)
            copy_out_act(act, "mb_k", 8)
            copy_out_act(act, "mb_v", 16, tokens=D)

            def out(h, o):
                rows = slice(64 * (h % 2), 64 * (h % 2) + 64)
                return A[rows, 24 + h // 2, :], o[rows, 0:T]
            attend_act(act, 16, A0["moba"], B0["moba"], 1, True, out)

        def moba_dve(dve, own):
            norm_dve(dve, "b2_1_in", xt, lambda t: vec("attn2", 8 + t), ht)
            rope_dve(dve, 4, moba_rope, ROPE)
            attend_dve(dve, own, 16, A0["moba"], B0["moba"], 1, True, 0.125)
            add_out_dve(dve, "mb_out")

        def moba_pool(pool, own):
            rope_pool(pool, own, 4, moba_rope, ROPE)

        FF0 = {0: 22, 1: 38}

        def mlp_pe(pe, l):
            norm_pe(pe, f"mlp{l}")
            linear_pe(pe, f"ff1_{l}", ht, ready=normed_ready(f"mlp{l}"))
            linear_pe(pe, f"ff2_{l}", tiles(0), ready=lambda e, kc: e.wait_ge(sem["ff_ready"], FF0[l] + kc // 2 + 1))

        def mlp_act(act, own, l):
            norm_act(act, f"mlp{l}", xt)
            copy_out_act(act, f"ff1_{l}", 0, ACT.Relu)

        def mlp_dve(dve, own, l):
            norm_dve(dve, f"mlp{l}", xt, lambda t: vec("mlp2", 8 * l + t), ht)
            add_out_dve(dve, f"ff2_{l}")

        def mlp_pool(pool, own, l):
            for p in range(16):
                wait_evac(pool, f"ff1_{l}", p)
                f = A[:, 2 * p:2 * p + 2, :]
                nc.gpsimd.tensor_tensor(f, f, f, ALU.mult).then_inc(sem["ff_ready"], 1)

        def ple_pe(pe, l):
            norm_pe(pe, f"ple{l}")
            linear_pe(pe, f"gate{l}", ht, ready=normed_ready(f"ple{l}"))
            wait_load(pe, f"p{l}")
            linear_pe(pe, f"proj{l}", tiles(8))

        def ple_act(act, own, l):
            norm_act(act, f"ple{l}", xt)
            copy_out_act(act, f"gate{l}", 0, ACT.Sigmoid)

        def ple_dve(dve, own, l):
            norm_dve(dve, f"ple{l}", xt, lambda t: vec("ple2", 8 * l + t), ht)
            for p in range(4):
                b = wait_pair(dve, f"proj{l}", p)
                wait_evac(dve, f"gate{l}", p)
                g, x, t = A[:, 2 * p:2 * p + 2, :], X[:, 2 * p:2 * p + 2, :], A[:, 10 + 2 * (p % 2):12 + 2 * (p % 2), :]
                nc.vector.tensor_tensor(t, g, bank(b), ALU.mult).then_inc(evac[b], 1)
                wait_evac(dve, f"proj{l}", p)
                own(nc.vector.tensor_tensor(x, x, t, ALU.add))

        def ple_pool(pool, own, l):
            load_pool(pool, A[:, 8:10, :], io["p"][l])

        HQ, HK, HV, HG, HB, HE, HM, HATT = 0, 8, 16, 24, 32, 40, 56, 64
        HSCALE = 128 ** -0.5
        MX, LBA, LBB, LBS, LB, OMLB = (SC[:, 24 + 8 * k:32 + 8 * k] for k in range(6))
        masks = flat(HM, 4).rearrange("p (l t) -> p l t", l=8)
        att = flat(HATT, 12).rearrange("p (h c) -> p h c", c=384)
        HALVES = [128, 64, 32, 16, 8, 4, 2, 1]
        LEVELS = len(HALVES) + 1

        def sides(base, m, side):
            v = flat(base, 8).rearrange("p (b s m) -> p b s m", s=2, m=m)
            return v[:, :, side, :]

        def reference_of(m):
            return sides(HB, m, 0)[:, :, m - 1:m].broadcast_to([P, 1024 // m, m])

        def hgrn_pe(pe):
            norm_pe(pe, "b3_in")
            linear_pe(pe, "hq", ht, ready=normed_ready("b3_in"))
            linear_pe(pe, "hf", ht)
            linear_pe(pe, "hi", ht, tokens=True)
            linear_pe(pe, "hg", ht)
            for p in range(4):
                wait_evac(pe, "hg", p)
            for i in range(LEVELS):
                base = 4 * (i % 2)
                if i < LEVELS - 1:
                    pe.wait_ge(sem["q_side"], i + 1)
                    pe.wait_ge(sem["k_side"], i + 1)
                if i >= 2:
                    pe.wait_ge(sem["lev_taken"], i - 1)
                e = HE + 8 * (i % 2)
                if i == 0:
                    for h in range(8):
                        mm = nc.tensor.matmul(PB[base + h // 4][:, h % 4 * P:h % 4 * P + P], A[:, e + h, 0:P],
                                              A[:, e + h, P:T], start=True, stop=True)
                else:
                    for n in range(16):
                        cols = slice(n % 2 * P, n % 2 * P + P)
                        if i < LEVELS - 1:
                            l, r = A[:, e + n // 2, cols], A[:, e + n // 2, cols]
                        else:
                            l, r = A[:, HK + n // 2, cols], A[:, HQ + n // 2, cols]
                        mm = nc.tensor.matmul(PB[base + n // 4][:, n % 4 * P:n % 4 * P + P], l, r, start=True, stop=True)
                mm.then_inc(sem["lev_mm"], 1)
            pe.wait_ge(sem["lev_taken"], LEVELS)
            v = flat(HV, 8).rearrange("p (m n) -> p m n", m=2)
            for h in range(8):
                o = PB[h // 2][:, h % 2 * T:h % 2 * T + T]
                nc.tensor.matmul(o, v[:, 0, h * P:h * P + P], att[:, h, 0:T], start=True, stop=False)
                mm = nc.tensor.matmul(o[:, P:T], v[:, 1, h * P:h * P + P], att[:, h, T:384], start=False, stop=True)
                if h % 2:
                    mm.then_inc(sem["ho_mm"], 1)
            headnorm_pe(pe, 2, 4)

        def hgrn_act(act, own):
            norm_act(act, "b3_in", xt)
            act.wait_ge(sem["lb_ready"], 1)
            nc.scalar.activation(SC[:, 32:48], SC[:, 32:48], ACT.Exp).then_inc(sem["lbs"], 1)
            copy_out_act(act, "hq", HQ, ACT.Silu)
            copy_out_act(act, "hf", HE, ACT.Sigmoid)
            copy_out_act(act, "hi", HV, tokens=D)
            copy_out_act(act, "hg", HG, ACT.Silu)
            for p in range(4):
                f = A[:, HE + 2 * p:HE + 2 * p + 2, :]
                act.wait_ge(sem["kf_ready"], p + 1)
                nc.scalar.activation(f, f, ACT.Ln).then_inc(sem["b_ready"], 1)
            for i in range(LEVELS - 1):
                e = flat(HE + 8 * (i % 2), 8)
                act.wait_ge(sem["d_ready"], i + 1)
                act.wait_ge(sem["sq_q"], i + 1)
                for k in range(2):
                    ins = nc.scalar.activation(e[:, 1024 * k:1024 * k + 1024], e[:, 1024 * k:1024 * k + 1024], ACT.Exp)
                ins.then_inc(sem["lev_exp"], 1)
            for q in range(4):
                act.wait_ge(sem["ho_mm"], q + 1)
                nc.scalar.activation(flat(HQ + 2 * q, 2), PB[q][:, :], ACT.Identity).then_inc(sem["ho_evac"], 1)
            headnorm_act(act, 2, pair_tiles(HQ, 4), lambda e, q: e.wait_ge(sem["ho_evac"], q + 1))

        def hgrn_dve(dve, own):
            norm_dve(dve, "b3_in", xt, lambda t: vec("attn3", t), ht)
            own(nc.vector.tensor_tensor(MX, vec("hg_lb", 0, 8), vec("hg_lb", 8, 8), ALU.max))
            own.wait()
            for k in range(2):
                ins = nc.vector.tensor_tensor(SC[:, 32 + 8 * k:40 + 8 * k], vec("hg_lb", 8 * k, 8), MX, ALU.subtract)
            ins.then_inc(sem["lb_ready"], 1)
            dve.wait_ge(sem["lbs"], 1)
            own(nc.vector.tensor_tensor(LBS, LBA, LBB, ALU.add))
            own.wait()
            own(nc.vector.reciprocal(LBS, LBS))
            own.wait()
            own(nc.vector.tensor_tensor(LB, LBA, LBS, ALU.mult))
            own.wait()
            own(nc.vector.tensor_scalar(OMLB, LB, -1.0, 1.0, ALU.mult, ALU.add))
            own.wait()
            for p in range(4):
                wait_evac(dve, "hf", p)
                for j in range(2):
                    t = 2 * p + j
                    own(nc.vector.tensor_scalar(A[:, HE + t, :], A[:, HE + t, :], OMLB[:, t:t + 1], LB[:, t:t + 1],
                                                ALU.mult, ALU.add))
                own.wait()
                for j in range(2):
                    t = 2 * p + j
                    ins = nc.vector.tensor_scalar(A[:, HK + t, :], A[:, HE + t, :], -HSCALE, HSCALE, ALU.mult, ALU.add)
                ins.then_inc(sem["kf_ready"], 1)
            dve.wait_ge(sem["hg_fg"], 1)
            for t in range(8):
                dve.wait_ge(sem["b_ready"], t // 2 + 1)
                ins = nc.vector.tensor_tensor_scan(A[:, HB + t, :], A[:, HM + 4, :], A[:, HE + t, :], 0.0, ALU.mult, ALU.add)
            ins.then_inc(sem["hg_sig"], 1)
            dve.wait_ge(sem["hg_sig"], 1)
            for i in range(LEVELS + 2):
                if i < LEVELS - 1:
                    m, e = HALVES[i], HE + 8 * (i % 2)
                    if i >= 2:
                        dve.wait_ge(sem["lev_mm"], i - 1)
                    nc.vector.tensor_tensor(sides(e, m, 1), sides(HB, m, 1), reference_of(m),
                                            ALU.subtract).then_inc(sem["d_ready"], 1)
                if 1 <= i < LEVELS:
                    j = i - 1
                    m, e = HALVES[j], HE + 8 * (j % 2)
                    dve.wait_ge(sem["lev_exp"], j + 1)
                    nc.vector.tensor_tensor(sides(e, m, 1), sides(e, m, 1), sides(HQ, m, 1), ALU.mult).then_inc(sem["q_side"], 1)
                if i >= 2:
                    j = i - 2
                    base = 4 * (j % 2)
                    dve.wait_ge(sem["lev_mm"], j + 1)
                    if j == 0:
                        for k in range(2):
                            ins = nc.vector.tensor_copy(att[:, 4 * k:4 * k + 4, P:T],
                                                        PB[base + k][:, :].rearrange("p (h t) -> p h t", h=4))
                    else:
                        if j == 1:
                            wait_load(dve, "levels")
                        else:
                            dve.wait_ge(sem["lev_taken"], j)
                        mask = (masks[:, j - 1, :] if j < LEVELS - 1 else ident).unsqueeze(1).broadcast_to([P, 2, P])
                        for k in range(4):
                            for hh in range(2):
                                to = att[:, 2 * k + hh, :].rearrange("p (z t) -> p z t", z=3)[:, 0:3:2, :]
                                of = PB[base + k][:, T * hh:T * hh + T].rearrange("p (z t) -> p z t", z=2)
                                if j == 1:
                                    ins = nc.vector.tensor_tensor(to, of, mask, ALU.mult)
                                else:
                                    ins = nc.vector.copy_predicated(to, mask.bitcast(I32), of)
                    ins.then_inc(sem["lev_taken"], 1)
            headnorm_dve(dve, own, 2, pair_tiles(HQ, 4), vec("hg_on", 0), after=lambda q: flat(HG + 2 * q, 2))

        def hgrn_pool(pool, own):
            pool.wait_ge(sem["stat_ready"], NORM["b3_in"][0] + 1)
            load_pool(pool, flat(HM, 4)[:, 0:7 * P], io["levels"])
            nc.gpsimd.memset(A[:, HM + 4, :], 1.0).then_inc(sem["hg_fg"], 1)
            pool.wait_ge(sem["hg_sig"], 1)
            for i in range(LEVELS):
                if i < LEVELS - 1:
                    m, e = HALVES[i], HE + 8 * (i % 2)
                    if i >= 2:
                        pool.wait_ge(sem["lev_mm"], i - 1)
                    nc.gpsimd.tensor_tensor(sides(e, m, 0), reference_of(m), sides(HB, m, 0),
                                            ALU.subtract).then_inc(sem["sq_q"], 1)
                if i >= 1:
                    j = i - 1
                    m, e = HALVES[j], HE + 8 * (j % 2)
                    pool.wait_ge(sem["lev_exp"], j + 1)
                    nc.gpsimd.tensor_tensor(sides(e, m, 0), sides(e, m, 0), sides(HK, m, 0), ALU.mult).then_inc(sem["k_side"], 1)

        LAT, QN, QR, KN, MV = 8, 14, 22, 26, 48
        lat_q, lat_kv = tiles(LAT), tiles(LAT + 3)
        mla_rope = pair_tiles(QR, 2) + [A[:, LAT + 5:LAT + 6, :]]

        def mla_pe(pe):
            linear_pe(pe, "lat", ht)
            norm_pe(pe, "qn")
            norm_pe(pe, "kn")
            linear_pe(pe, "uqn", lat_q, ready=normed_ready("qn"))
            linear_pe(pe, "uqr", lat_q)
            linear_pe(pe, "uk", lat_kv, ready=normed_ready("kn"))
            linear_pe(pe, "uv", lat_kv, tokens=True)
            rope_pe(pe, 12, mla_rope, rot3, lambda e, k: wait_evac(e, "uqr", k) if k < 2 else wait_evac(e, "lat", 2))
            for p in range(4):
                wait_evac(pe, "uv", p)
            pe.wait_ge(sem["rope_done"], 15)

            def parts(h, c):
                rows = slice(64 * (h % 2), 64 * (h % 2) + 64)
                return [(A[:, QN + h, :], A[:, KN + h, :]), (A[rows, QR + h // 2, :], A[rows, LAT + 5, :])]
            v = flat(MV, 8).rearrange("p (m n) -> p m n", m=2)
            attend_pe(pe, 8, A0["mla"], B0["mla"], 1, True, scores_causal(parts),
                      pv_causal(lambda h, m: v[:, m, h * P:h * P + P], lambda h: slice(0, P)))

        def mla_act(act, own):
            tables_act(act, 1)
            copy_out_act(act, "lat", LAT)
            norm_act(act, "qn", lat_q, lambda e, t: wait_evac(e, "lat", t // 2))
            norm_act(act, "kn", lat_kv, lambda e, t: wait_evac(e, "lat", (t + 3) // 2))
            copy_out_act(act, "uqn", QN)
            copy_out_act(act, "uqr", QR)
            copy_out_act(act, "uk", KN)
            copy_out_act(act, "uv", MV, tokens=D)
            attend_act(act, 8, A0["mla"], B0["mla"], 1, True, lambda h, o: (A[:, QN + h, :], o[:, 0:T]))

        def mla_dve(dve, own):
            tables_dve(dve, own, "pos3", vec("inv3", 0))
            norm_dve(dve, "qn", lat_q, lambda t: vec("mla_qn", t), lat_q)
            norm_dve(dve, "kn", lat_kv, lambda t: vec("mla_kn", t), lat_kv)
            dve.wait_ge(sem["sincos"], 4)
            rope_dve(dve, 12, mla_rope, 34)
            attend_dve(dve, own, 8, A0["mla"], B0["mla"], 1, True, 192 ** -0.5)

        def mla_pool(pool, own):
            load_pool(pool, A[:, 40, :].bitcast(I32), io["pos3"])
            pool.wait_ge(sem["sincos"], 4)
            rope_pool(pool, own, 12, mla_rope, 34)

        def merge_pe(pe):
            linear_pe(pe, "ga", ht)
            linear_pe(pe, "bra", tiles(0))
            linear_pe(pe, "gb", ht)
            linear_pe(pe, "brb", tiles(QN))
            linear_pe(pe, "wout", tiles(38), ready=lambda e, kc: e.wait_ge(sem["oa_ready"], kc // 2 + 1))

        def merge_act(act, own):
            copy_out_act(act, "ga", 22, ACT.Sigmoid)
            copy_out_act(act, "gb", 30, ACT.Sigmoid)

        def merge_dve(dve, own):
            for p in range(4):
                wait_evac(dve, "ga", p)
                b = wait_pair(dve, "bra", p)
                nc.vector.tensor_tensor(A[:, 38 + 2 * p:40 + 2 * p, :], bank(b), A[:, 22 + 2 * p:24 + 2 * p, :],
                                        ALU.mult).then_inc(evac[b], 1)
            for p in range(4):
                wait_evac(dve, "gb", p)
                b = wait_pair(dve, "brb", p)
                if p >= 2:
                    dve.wait_ge(sem["oa_ready"], p - 1)
                nc.vector.tensor_tensor(A[:, 46 + 2 * (p % 2):48 + 2 * (p % 2), :], bank(b), A[:, 30 + 2 * p:32 + 2 * p, :],
                                        ALU.mult).then_inc(evac[b], 1)
                wait_evac(dve, "brb", p)
                y = A[:, 38 + 2 * p:40 + 2 * p, :]
                nc.vector.tensor_tensor(y, y, A[:, 46 + 2 * (p % 2):48 + 2 * (p % 2), :], ALU.add).then_inc(sem["oa_ready"], 1)
            add_out_dve(dve, "wout")

        WR = flat(0, 3)[:, 0:576].rearrange("p (k n) -> p k n", k=8)
        RB = flat(0, 3)[:, 576:648]
        small3 = flat(3, 4)
        _at = [0]

        def tmp(*shape):
            n = math.prod(shape)
            a = small3[:, _at[0]:_at[0] + n]
            _at[0] += n
            if len(shape) == 2:
                return a.rearrange("p (a b) -> p a b", a=shape[0])
            if len(shape) == 3:
                return a.rearrange("p (a b c) -> p a b c", a=shape[0], b=shape[1])
            return a
        LOG = tmp(2, 72)
        PROD = tmp(2, 8, 8)
        GD, GE_, GF, GOH, ESEL, ED, EF, OH1, OH2, EM, WE, WE2 = (tmp(2, 8) for _ in range(12))
        GMAX, GSUM, GIDX, M1, I1, M2, I2, RAT, W1_, W2_ = (tmp(2, 1) for _ in range(10))
        SLOTN = 64
        EPAD = NEXP + 4
        WTE = A[:, 7, 0:2 * EPAD].rearrange("p (c e) -> p c e", c=2)
        RANK = A[:, 24, 0:2 * EPAD].rearrange("p (c e) -> p c e", c=2)
        SEL = A[:, 31, 0:128].rearrange("p (c e) -> p c e", c=2)
        CMAX = A[:, 31, 128:129]
        FITS = A[:, 31, 129:130].bitcast(I32)
        SILU, HID, ACC = 8, 12, 16
        acc = flat(ACC, 8).rearrange("p (c n) -> p c n", c=2)

        def per8(a):
            return a.broadcast_to([P, 2, 8])

        iota8 = CT[:, CON["iota"]:CON["iota"] + 8].unsqueeze(1).broadcast_to([P, 2, 8])

        def first_of(own, d, f, idx, onehot):
            own(nc.vector.tensor_scalar(f, d, 0.0, 100.0, ALU.is_lt, ALU.mult))
            own.wait()
            own(nc.vector.tensor_tensor(f, f, iota8, ALU.add))
            own.wait()
            own(nc.vector.tensor_reduce(idx, f, AX.X, ALU.min))
            own.wait()
            own(nc.vector.tensor_tensor(onehot, iota8, per8(idx), ALU.is_equal))
            own.wait()

        def router_dve(dve, own):
            dve.wait_ge(sem["rt_mm"], 1)
            own(nc.vector.tensor_tensor(LOG, PB[0][:, 0:144].rearrange("p (c n) -> p c n", c=2),
                                        RB.unsqueeze(1).broadcast_to([P, 2, 72]), ALU.add))
            own.wait()
            own(nc.vector.tensor_reduce(GMAX, LOG[:, :, 0:8], AX.X, ALU.max))
            own.wait()
            own(nc.vector.tensor_tensor(GD, LOG[:, :, 0:8], per8(GMAX), ALU.subtract))
            own.wait()
            first_of(own, GD, GF, GIDX, GOH)
            for c in range(2):
                own(nc.vector.tensor_tensor(PROD[:, c], LOG[:, c, 8:72].rearrange("p (g e) -> p g e", g=8),
                                            GOH[:, c, :].unsqueeze(2).broadcast_to([P, 8, 8]), ALU.mult))
            own.wait()
            for c in range(2):
                own(nc.vector.tensor_reduce(ESEL[:, c], PROD[:, c].rearrange("p g e -> p e g"), AX.X, ALU.add))
            own.wait()
            own(nc.vector.tensor_reduce(M1, ESEL, AX.X, ALU.max))
            own.wait()
            own(nc.vector.tensor_tensor(ED, ESEL, per8(M1), ALU.subtract))
            own.wait()
            first_of(own, ED, EF, I1, OH1)
            own(nc.vector.scalar_tensor_tensor(out=EM, in0=OH1, scalar=-BIG, in1=ESEL, op0=ALU.mult, op1=ALU.add))
            own.wait()
            own(nc.vector.tensor_reduce(M2, EM, AX.X, ALU.max))
            own.wait()
            own(nc.vector.tensor_tensor(ED, EM, per8(M2), ALU.subtract))
            own.wait()
            first_of(own, ED, EF, I2, OH2)
            nc.vector.tensor_tensor(RAT, M2, M1, ALU.subtract).then_inc(sem["rt_log"], 1)
            dve.wait_ge(sem["rt_exp"], 1)
            own(nc.vector.tensor_reduce(GSUM, GE_, AX.X, ALU.add))
            own(nc.vector.tensor_scalar(W1_, RAT, 1.0, None, ALU.add))
            own.wait()
            own(nc.vector.tensor_tensor(W1_, W1_, GSUM, ALU.mult))
            own.wait()
            own(nc.vector.reciprocal(W1_, W1_))
            own.wait()
            own(nc.vector.tensor_tensor(W2_, W1_, RAT, ALU.mult))
            own(nc.vector.tensor_tensor(WE, OH1, per8(W1_), ALU.mult))
            own.wait()
            own(nc.vector.tensor_tensor(WE2, OH2, per8(W2_), ALU.mult))
            own.wait()
            own(nc.vector.tensor_tensor(WE, WE, WE2, ALU.add))
            own.wait()
            own(nc.vector.tensor_tensor(WE2, OH1, OH2, ALU.add))
            own(nc.vector.memset(WTE, 0.0))
            own(nc.vector.memset(RANK, -1.0))
            own.wait()
            for c in range(2):
                for to, of in ((WTE[:, c, 0:NEXP], WE), (SEL[:, c, :], WE2)):
                    ins = nc.vector.tensor_tensor(to.rearrange("p (g e) -> p g e", g=8),
                                                  GOH[:, c, :].unsqueeze(2).broadcast_to([P, 8, 8]),
                                                  of[:, c, :].unsqueeze(1).broadcast_to([P, 8, 8]), ALU.mult)
            ins.then_inc(sem["wt_ready"], 1)
            dve.wait_ge(sem["rank_mm"], 1)
            own(nc.vector.tensor_tensor(SEL, PB[1][:, 0:128].rearrange("p (c e) -> p c e", c=2), SEL, ALU.mult))
            own(nc.vector.tensor_reduce(CMAX, PB[1][:, 128:192], AX.X, ALU.max))
            own.wait()
            own(nc.vector.tensor_scalar(RANK[:, :, 0:NEXP], SEL, -1.0, None, ALU.add))
            nc.vector.tensor_copy(FITS, CMAX).then_inc(sem["fits_ready"], 1)
            dve.wait_ge(sem["fits_ready"], 1)
            own.wait()

        def expert_slot(e, j):
            u = DENSE_UNITS + EXPERT_UNITS * e + j
            return u % SLOTS, 16 * (u // SLOTS + 1)

        def moe_pe(pe):
            norm_pe(pe, "ffn3")
            pe.wait_ge(sem["normed"], NORM["ffn3"][2] + 8)
            wait_load(pe, "router")
            for c in range(2):
                for k in range(8):
                    mm = nc.tensor.matmul(PB[0][:, 72 * c:72 * c + 72], H[:, k, c * P:c * P + P], WR[:, k, :],
                                          start=(k == 0), stop=(k == 7))
            mm.then_inc(sem["rt_mm"], 1)
            pe.wait_ge(sem["wt_ready"], 1)
            nc.tensor.matmul(PB[1][:, 0:64], upto, SEL[:, 0, :], start=True, stop=True)
            nc.tensor.matmul(PB[1][:, 64:128], ones, SEL[:, 0, :], start=True, stop=False)
            nc.tensor.matmul(PB[1][:, 64:128], upto, SEL[:, 1, :], start=False, stop=True)
            nc.tensor.matmul(PB[1][:, 128:192], ones, SEL[:, 0, :], start=True, stop=False)
            nc.tensor.matmul(PB[1][:, 128:192], ones, SEL[:, 1, :], start=False, stop=True).then_inc(sem["rank_mm"], 1)
            pe.wait_ge(sem["fits_ready"], 1)
            most = pe.value_load(FITS[0:1, :], min_val=0, max_val=T)
            with pe.If(most < SLOTN + 1):
                compact_pe(pe)
            with pe.Else():
                dense_pe(pe)
            norm_pe(pe, "final3")

        def moe_act(act, own):
            norm_act(act, "ffn3", xt)
            act.wait_ge(sem["rt_log"], 1)
            own(nc.scalar.activation(GE_, GD, ACT.Exp))
            nc.scalar.activation(RAT, RAT, ACT.Exp).then_inc(sem["rt_exp"], 1)
            act.wait_ge(sem["fits_ready"], 1)
            most = act.value_load(FITS[0:1, :], min_val=0, max_val=T)
            with act.If(most < SLOTN + 1):
                compact_act(act)
            with act.Else():
                dense_act(act)
            norm_act(act, "final3", xt, lambda en, t: en.wait_ge(sem["x_done"], t // 2 + 1))

        def moe_dve(dve, own):
            norm_dve(dve, "ffn3", xt, lambda t: vec("ffn3", t), ht)
            router_dve(dve, own)
            most = dve.value_load(FITS[0:1, :], min_val=0, max_val=T)
            with dve.If(most < SLOTN + 1):
                compact_dve(dve)
            with dve.Else():
                dense_dve(dve)
            norm_dve(dve, "final3", xt, lambda t: vec("final3", t), mix)

        def dense_pe(pe):
            with pe.Fori(0, NEXP // 2) as i:
                for e in range(2):
                    pe.wait_ge(sem["up_taken"], 4 * i + 2 * e + 1)
                    for j in range(4):
                        slot, first = expert_slot(e, j)
                        pe.wait_ge(arrived[slot], 16 * i + first)
                        for m in range(2):
                            for k in range(8):
                                mm = nc.tensor.matmul(PB[j][:, m * T:m * T + T], W[:, slot, k, m * P:m * P + P],
                                                      ht(k), start=(k == 0), stop=(k == 7))
                        mm.then_inc(sem["unit_used"], 1)
                    pe.wait_ge(sem["up_taken"], 4 * i + 2 * e + 3)
                    pe.wait_ge(sem["dn_taken"], 8 * i + 4 * e + 1)
                    for j in range(2):
                        slot, first = expert_slot(e, 4 + j)
                        pe.wait_ge(arrived[slot], 16 * i + first)
                        w = W[:, slot].rearrange("p a b -> p (a b)").rearrange("p (k n) -> p k n", k=4)
                        for c in range(2):
                            for k in range(4):
                                mm = nc.tensor.matmul(PB[4 + 2 * j + c][:, :], A[:, HID + k, c * P:c * P + P], w[:, k, :],
                                                      start=(k == 0), stop=(k == 3))
                        mm.then_inc(sem["unit_used"], 1)
            pe.wait_ge(sem["dn_taken"], 4 * NEXP + 1)
            for k in range(8):
                for c in range(2):
                    mm = nc.tensor.transpose(PB[k // 2][:, (k % 2) * T + c * P:(k % 2) * T + c * P + P],
                                             acc[:, c, k * P:k * P + P], ident)
                if k % 2:
                    mm.then_inc(sem["tr_mm"], 1)

        def dense_act(act):
            with act.Fori(0, NEXP // 2) as i:
                for e in range(2):
                    act.wait_ge(sem["up_taken"], 4 * i + 2 * e + 1)
                    for j in range(2):
                        act.wait_ge(sem["unit_used"], 2 * EXPERT_UNITS * i + (DENSE_UNITS + EXPERT_UNITS * e + j + 1))
                        nc.scalar.activation(flat(SILU + 2 * j, 2), PB[j][:, :], ACT.Silu).then_inc(sem["up_act"], 1)

        def dense_dve(dve):
            nc.vector.memset(flat(HID, 4), 0.0).then_inc(sem["up_taken"], 1)
            nc.vector.memset(flat(ACC, 8), 0.0).then_inc(sem["dn_taken"], 1)
            with dve.Fori(0, NEXP // 2) as i:
                for e in range(2):
                    for j in range(2):
                        dve.wait_ge(sem["up_act"], 4 * i + 2 * e + j + 1)
                        dve.wait_ge(sem["unit_used"], 2 * EXPERT_UNITS * i + (DENSE_UNITS + EXPERT_UNITS * e + j + 3))
                        nc.vector.tensor_tensor(flat(HID + 2 * j, 2), PB[2 + j][:, :], flat(SILU + 2 * j, 2),
                                                ALU.mult).then_inc(sem["up_taken"], 1)
                    dve.wait_ge(sem["dn_taken"], 8 * i + 4 * e + 1)
                    for j in range(2):
                        dve.wait_ge(sem["unit_used"], 2 * EXPERT_UNITS * i + (DENSE_UNITS + EXPERT_UNITS * e + j + 5))
                        for c in range(2):
                            a = acc[:, c, 512 * j:512 * j + 512]
                            nc.vector.scalar_tensor_tensor(out=a, in0=PB[4 + 2 * j + c][:, :],
                                                           scalar=WTE[:, c, bass.ds(2 * i + e, 1)], in1=a,
                                                           op0=ALU.mult, op1=ALU.add).then_inc(sem["dn_taken"], 1)
            for p in range(4):
                dve.wait_ge(sem["tr_mm"], p + 1)
                x = X[:, 2 * p:2 * p + 2, :]
                nc.vector.tensor_tensor(x, x, bank(p), ALU.add).then_inc(sem["x_done"], 1)

        PAIR = 2 * SLOTN
        CSILU, CHID = A[:, 8, :], A[:, 9, :].rearrange("p (k s) -> p k s", k=4)
        GSEL = A[:, 10, :].rearrange("p (c s) -> p c s", c=2)
        GWSEL = A[:, 11, :].rearrange("p (c s) -> p c s", c=2)
        GATHERED = flat(12, 4).rearrange("p (k s) -> p k s", k=8)
        HTOK = flat(16, 8).rearrange("p (c n) -> p c n", c=2)
        YEX = flat(25, 4)
        SPREAD = A[:, 29, :]
        ZERO = flat(32, 2)
        slots = CT[:, CON["iota"]:CON["iota"] + SLOTN]

        def gather_pe(pe):
            for k in range(8):
                for c in range(2):
                    mm = nc.tensor.matmul(PB[3 - k // 4][:, k % 4 * PAIR:(k % 4 + 1) * PAIR], HTOK[:, c, k * P:k * P + P],
                                          GSEL[:, c, :], start=(c == 0), stop=(c == 1))
                if k % 4 == 3:
                    mm.then_inc(sem["gather_mm"], 1)

        def scatter_pe(pe):
            for d in range(8):
                mm = nc.tensor.matmul(PB[4 + d // 2][:, d % 2 * T:d % 2 * T + T], YEX[:, d * P:d * P + P],
                                      SPREAD, start=False, stop=True, skip_group_check=True)
            mm.then_inc(sem["scattered"], 1)

        def compact_pe(pe):
            pe.wait_ge(sem["zero_in"], 1)
            for b in range(4):
                nc.tensor.matmul(PB[4 + b][:, :], ZERO[:, 0:P], ZERO, start=True, stop=True)
            for k in range(4):
                for j in range(4):
                    n = 4 * k + j
                    mm = nc.tensor.transpose(PB[k][:, j * P:j * P + P], H[:, n % 8, n // 8 * P:n // 8 * P + P], ident)
                mm.then_inc(sem["htok_mm"], 1)
            pe.wait_ge(sem["htok_ready"], 4)
            pe.wait_ge(sem["gsel_ready"], 1)
            gather_pe(pe)
            with pe.Fori(0, NEXP // 2) as i:
                pe.wait_ge(sem["xc_ready"], 2 * i + 2)
                pe.wait_ge(sem["spread_ready"], i + 1)
                for e in range(2):
                    for j in range(4):
                        slot, first = expert_slot(e, j)
                        pe.wait_ge(arrived[slot], 16 * i + first)
                        for m in range(2):
                            for k in range(8):
                                o = PB[e][:, (2 * j + m) * SLOTN:(2 * j + m) * SLOTN + SLOTN]
                                mm = nc.tensor.matmul(o, W[:, slot, k, m * P:m * P + P],
                                                      GATHERED[:, k, e * SLOTN:e * SLOTN + SLOTN],
                                                      start=(k == 0), stop=(k == 7))
                        mm.then_inc(sem["unit_used"], 1)
                    if e == 0:
                        pe.wait_ge(sem["y_out"], 4 * i + 1)
                        scatter_pe(pe)
                    else:
                        pe.wait_ge(sem["gsel_ready"], i + 2)
                        pe.wait_ge(sem["y_out"], 4 * i + 2)
                        gather_pe(pe)
                        pe.wait_ge(sem["y_out"], 4 * i + 3)
                        pe.wait_ge(sem["gwsel_ready"], i + 1)
                        for c in range(2):
                            mm = nc.tensor.matmul(PB[0][:, c * P:c * P + P], GWSEL[:, c, :], ident, start=True, stop=True)
                        mm.then_inc(sem["spread_mm"], 1)
                        pe.wait_ge(sem["xc_ready"], 2 * i + 3)
                    pe.wait_ge(sem["hid_ready"], 2 * i + e + 1)
                    for j in range(2):
                        slot, first = expert_slot(e, 4 + j)
                        pe.wait_ge(arrived[slot], 16 * i + first)
                        w = W[:, slot].rearrange("p a b -> p (a b)").rearrange("p (k n) -> p k n", k=4)
                        for k in range(4):
                            mm = nc.tensor.matmul(PB[e if j else 3][0:SLOTN, :], CHID[:, k, :], w[:, k, :],
                                                  start=(k == 0), stop=(k == 3))
                        mm.then_inc(sem["unit_used"], 1)
            pe.wait_ge(sem["y_out"], 2 * NEXP + 1)
            pe.wait_ge(sem["spread_ready"], NEXP // 2 + 1)
            scatter_pe(pe)
            pe.wait_ge(sem["x_done"], 4)

        def compact_act(act):
            for k in range(4):
                act.wait_ge(sem["htok_mm"], k + 1)
                nc.scalar.activation(flat(16 + 2 * k, 2), PB[k][:, :], ACT.Identity).then_inc(sem["htok_ready"], 1)
            with act.Fori(0, NEXP // 2) as i:
                for e in range(2):
                    used = 2 * EXPERT_UNITS * i + (DENSE_UNITS + EXPERT_UNITS * e)
                    act.wait_ge(sem["unit_used"], used + 4)
                    nc.scalar.activation(CSILU, PB[e][:, 0:T], ACT.Silu).then_inc(sem["silu_ready"], 1)
                    if e == 0:
                        act.wait_ge(sem["scattered"], i + 1)
                    else:
                        act.wait_ge(sem["spread_mm"], i + 1)
                        nc.scalar.activation(SPREAD, PB[0][:, 0:T], ACT.Identity).then_inc(sem["spread_ready"], 1)
                    for j in range(2):
                        act.wait_ge(sem["unit_used"], used + 5 + j)
                        nc.scalar.activation(YEX[e * SLOTN:e * SLOTN + SLOTN, 512 * j:512 * j + 512],
                                             PB[e if j else 3][0:SLOTN, :], ACT.Identity).then_inc(sem["y_out"], 1)

        def select_dve(pair):
            for e in range(2):
                for c in range(2):
                    ins = nc.vector.tensor_scalar(GSEL[:, c, e * SLOTN:e * SLOTN + SLOTN], slots,
                                                  RANK[:, c, bass.ds(2 * pair + e, 1)], None, ALU.is_equal)
            ins.then_inc(sem["gsel_ready"], 1)

        def weigh_dve(pair):
            for e in range(2):
                for c in range(2):
                    ins = nc.vector.tensor_scalar(GWSEL[:, c, e * SLOTN:e * SLOTN + SLOTN], slots,
                                                  RANK[:, c, bass.ds(2 * pair + e, 1)],
                                                  WTE[:, c, bass.ds(2 * pair + e, 1)], ALU.is_equal, ALU.mult)
            ins.then_inc(sem["gwsel_ready"], 1)

        def gathered_dve(dve, half):
            nc.vector.tensor_copy(flat(12 + 2 * half, 2), PB[3 - half][:, :]).then_inc(sem["xc_ready"], 1)

        def compact_dve(dve):
            nc.vector.memset(ZERO, 0.0).then_inc(sem["zero_in"], 1)
            nc.vector.memset(YEX, 0.0).then_inc(sem["y_out"], 1)
            nc.vector.memset(SPREAD, 0.0).then_inc(sem["spread_ready"], 1)
            select_dve(0)
            weigh_dve(0)
            for half in range(2):
                dve.wait_ge(sem["gather_mm"], half + 1)
                gathered_dve(dve, half)
            select_dve(1)
            with dve.Fori(0, NEXP // 2) as i:
                for e in range(2):
                    dve.wait_ge(sem["silu_ready"], 2 * i + e + 1)
                    nc.vector.tensor_tensor(CHID.rearrange("p k s -> p (k s)"), PB[e][:, T:2 * T], CSILU,
                                            ALU.mult).then_inc(sem["hid_ready"], 1)
                for half in range(2):
                    dve.wait_ge(sem["gather_mm"], 2 * i + half + 3)
                    gathered_dve(dve, half)
                select_dve(i + 2)
                dve.wait_ge(sem["spread_mm"], i + 1)
                weigh_dve(i + 1)
            dve.wait_ge(sem["scattered"], NEXP // 2 + 1)
            for p in range(4):
                x = X[:, 2 * p:2 * p + 2, :]
                nc.vector.tensor_tensor(x, x, bank(4 + p), ALU.add).then_inc(sem["x_done"], 1)

        def moe_pool(pool, own):
            load_pool(pool, flat(0, 3)[:, 0:648], io["router"])

        block = ctx.enter_context(nc.Block())

        @block.sync
        def _(sp):
            sp.dma_start(X[:, :, :], io["x"]).then_inc(sem["x_in"], 16)
            sp.dma_start(VT[:, :], io["vec"]).then_inc(sem["vec_in"], 16)
            sp.dma_start(CT[:, :], io["con"]).then_inc(sem["vec_in"], 16)

            def load(u, slot):
                dst = W[:, slot].rearrange("p a b -> p (a b)")
                sp.dma_start(dst, io["stream"][u]).then_inc(arrived[slot], 16)
            for s in range(SLOTS):
                load(s, s)
            with sp.Fori(0, UNITS // SLOTS - 1) as i:
                for s in range(SLOTS):
                    sp.wait_ge(sem["unit_used"], SLOTS * i + s + 1)
                    dst = W[:, s].rearrange("p a b -> p (a b)")
                    sp.dma_start(dst, io["stream"][bass.ds(SLOTS * i + (SLOTS + s), 1)].rearrange("u p n -> (u p) n")
                                 ).then_inc(arrived[s], 16)
            for s in range(UNITS % SLOTS):
                u = UNITS // SLOTS * SLOTS + s
                sp.wait_ge(sem["unit_used"], u - SLOTS + 1)
                load(u, s)
            sp.wait_ge(sem["normed"], NORM["final3"][2] + 8)
            sp.dma_start(io["out"], A[:, MIX:MIX + 8, :]).then_inc(sem["out_written"], 16)
            sp.wait_ge(sem["out_written"], 16)

        @block.tensor
        def _(pe):
            for step in (ssm_in_pe, ssm_core_pe, ssm_out_pe):
                step(pe)
                meet("pe", pe)
            xattn_pe(pe, 0)
            meet("pe", pe)
            ffn_pe(pe, 0)
            meet("pe", pe)
            conf_pe(pe)
            meet("pe", pe)
            xattn_pe(pe, 1)
            meet("pe", pe)
            ffn_pe(pe, 1)
            meet("pe", pe)
            for l, mixer in enumerate((even_pe, moba_pe)):
                mixer(pe)
                meet("pe", pe)
                mlp_pe(pe, l)
                meet("pe", pe)
                ple_pe(pe, l)
                meet("pe", pe)
            norm_pe(pe, "final2")
            meet("pe", pe)
            for step in (hgrn_pe, mla_pe, merge_pe):
                step(pe)
                meet("pe", pe)
            moe_pe(pe)

        def compute(eng, who, own, s):
            for step in s["ssm"]:
                step(eng, own)
                meet(who, eng)
            s["xattn"](eng, own, 0)
            meet(who, eng)
            s["ffn"](eng, own, 0)
            meet(who, eng)
            s["conf"](eng, own)
            meet(who, eng)
            s["xattn"](eng, own, 1)
            meet(who, eng)
            s["ffn"](eng, own, 1)
            meet(who, eng)
            for l, mixer in enumerate(s["mixers"]):
                mixer(eng, own)
                meet(who, eng)
                s["mlp"](eng, own, l)
                meet(who, eng)
                s["ple"](eng, own, l)
                meet(who, eng)
            s["final2"](eng)
            meet(who, eng)
            for step in s["block3"]:
                step(eng, own)
                meet(who, eng)
            s["moe"](eng, own)

        @block.scalar
        def _(act):
            compute(act, "act", Own(act, sem["own_act"]), dict(
                ssm=(ssm_in_act, ssm_core_act, ssm_out_act), xattn=xattn_act, ffn=ffn_act, conf=conf_act,
                mixers=(even_act, moba_act), mlp=mlp_act, ple=ple_act, final2=lambda e: norm_act(e, "final2", xt),
                block3=(hgrn_act, mla_act, merge_act), moe=moe_act))

        @block.vector
        def _(dve):
            compute(dve, "dve", Own(dve, sem["own_dve"]), dict(
                ssm=(ssm_in_dve, ssm_core_dve, ssm_out_dve), xattn=xattn_dve, ffn=ffn_dve, conf=conf_dve,
                mixers=(even_dve, moba_dve), mlp=mlp_dve, ple=ple_dve,
                final2=lambda e: norm_dve(e, "final2", xt, lambda t: vec("final2", t), xt),
                block3=(hgrn_dve, mla_dve, merge_dve), moe=moe_dve))

        @block.gpsimd
        def _(pool):
            compute(pool, "pool", Own(pool, sem["own_pool"]), dict(
                ssm=(ssm_in_pool, ssm_core_pool, ssm_out_pool), xattn=xattn_pool, ffn=ffn_pool, conf=conf_pool,
                mixers=(even_pool, moba_pool), mlp=mlp_pool, ple=ple_pool, final2=lambda e: None,
                block3=(hgrn_pool, mla_pool, lambda e, o: None), moe=moe_pool))


def constants():
    c = np.zeros((P, NCON), np.float32)
    r, k = np.arange(P)[:, None], np.arange(P)[None, :]
    c[:, 0:128] = r == k
    c[:, 128:256] = 1
    c[:, 256:384] = r <= k
    c[:, 384:512] = r >= k
    for at, half in ((CON["rot2"], 8), (CON["rot3"], 32)):
        for m in range(P):
            d = m % 64
            if d < half:
                c[m + half, at + m] = -1
            elif d < 2 * half:
                c[m - half, at + m] = 1
    hide = np.where(k <= r, 0, -BIG)
    c[:, CON["cmask"]:CON["cmask"] + 128] = hide
    c[:, CON["cmask"] + 256:CON["cmask"] + 384] = hide
    c[:, CON["iota"]:CON["iota"] + 64] = np.arange(64)
    strict = np.zeros((P, 768), np.float32)
    q = np.arange(T)[None, :]
    strict[:, 0:T] = r < q
    strict[:, T:384] = r < k
    strict[:, 384:768] = (strict[:, 0:384] - 1) * BIG
    levels = np.concatenate([((r // (2 * m) == k // (2 * m)) & (r % (2 * m) < m) & (k % (2 * m) >= m))
                             for m in (64, 32, 16, 8, 4, 2, 1)], 1).astype(np.float32)
    freq = np.zeros((P, 2), np.float32)
    for j, (half, theta, rot) in enumerate(((8, 500000.0, 16), (32, 10000.0, 64))):
        for m in range(P):
            d = m % 64
            if d < 2 * half:
                freq[m, j] = np.float32(theta) ** (-np.float32((d % half) / half))
    return c, strict, levels, freq


def columns(a):
    a = np.asarray(a)
    a = a.reshape(-1, a.shape[-1])
    return np.concatenate([v.reshape(-1, P).T for v in a], 1)


def stream(inp):
    out = np.zeros((UNITS, P, UNIT), np.float32)
    w_in, uq, ukv = inp["w_in_3"][0], inp["mla_w_uq_3"][0], inp["mla_w_ukv_3"][0]
    cuts = np.cumsum([0, 1024, 1024, 1024, 1024, 384, 256, 64, 1024, 1024])
    part = lambda k: w_in[:, cuts[k]:cuts[k + 1]]
    uqh, ukh = uq.reshape(384, 8, 192), ukv.reshape(256, 8, 256)
    ab, mb = inp["ab_w_in_2"][0], inp["moba_w_in_2"][0]
    pw1 = inp["cf_pw1_w"][0]

    def woven(first, second):
        n = first.shape[1] // T
        return np.concatenate([m[:, T * k:T * k + T] for k in range(n) for m in (first, second)], 1)
    mats = {
        "ssm_x": inp["ssm_in_w"][0][:, 2048:5120], "ssm_z": inp["ssm_in_w"][0][:, 0:2048], "ssm_out": inp["ssm_out_w"][0],
        "pw1": woven(pw1[:, D:], pw1[:, :D]), "pw2": inp["cf_pw2_w"][0],
        "ab_aq": ab[:, 0:512], "ab_ak": ab[:, 512:1024], "ab_av": ab[:, 1024:1536],
        "ab_bq": ab[:, 1536:2048], "ab_bk": ab[:, 2048:2560], "ab_bv": ab[:, 2560:3072], "ab_out": inp["ab_w_out_2"][0],
        "mb_q": mb[:, 0:D], "mb_k": mb[:, D:2 * D], "mb_v": mb[:, 2 * D:], "mb_out": inp["moba_w_out_2"][0],
        "hq": part(0), "hf": part(1), "hi": part(2), "hg": part(3),
        "lat": np.concatenate([part(4), part(5), part(6), part(6)], 1),
        "uqn": uqh[:, :, :128].reshape(384, 1024), "uqr": uqh[:, :, 128:].reshape(384, 512),
        "uk": ukh[:, :, :128].reshape(256, 1024), "uv": ukh[:, :, 128:].reshape(256, 1024),
        "ga": part(7), "bra": inp["w_branch_hgrn_3"][0], "gb": part(8), "brb": inp["w_branch_mla_3"][0],
        "wout": inp["w_out_3"][0],
    }
    for l in range(2):
        mats[f"xa_k{l}"], mats[f"xa_v{l}"] = inp["xa_kv_w"][l][:, :D], inp["xa_kv_w"][l][:, D:]
        mats[f"xa_q{l}"], mats[f"xa_o{l}"] = inp["xa_q_w"][l], inp["xa_o_w"][l]
        mats[f"ffn_in{l}"] = woven(inp["ffn_in_w"][l][:, :DFF], inp["ffn_in_w"][l][:, DFF:])
        mats[f"ffn_out{l}"] = inp["ffn_out_w"][l]
        mats[f"ff1_{l}"], mats[f"ff2_{l}"] = inp["w_ff1_2"][l], inp["w_ff2_2"][l]
        mats[f"gate{l}"], mats[f"proj{l}"] = inp["ple_gate_2"][l], inp["ple_proj_2"][l]
    for name, (chunks, pairs, share, unit, _) in LIN.items():
        m = mats[name].reshape(chunks, P, pairs, T)
        for p in range(pairs):
            if share == 1:
                for j in range(-(-chunks // 8)):
                    part_ = m[8 * j:8 * j + 8, :, p, :]
                    out[unit_of(name, p, 8 * j), :, 0:part_.shape[0] * T] = part_.transpose(1, 0, 2).reshape(P, -1)
            else:
                at = p % share * chunks * T
                out[unit_of(name, p, 0), :, at:at + chunks * T] = m[:, :, p, :].transpose(1, 0, 2).reshape(P, -1)
    ex = out[DENSE_UNITS:].reshape(NEXP, EXPERT_UNITS, P, UNIT)
    for e in range(NEXP):
        for k, w in enumerate((inp["expert_w1_3"][0, e], inp["expert_w3_3"][0, e])):
            ex[e, 2 * k:2 * k + 2] = w.reshape(8, P, 2, T).transpose(2, 1, 0, 3).reshape(2, P, UNIT)
        ex[e, 4:6] = inp["expert_w2_3"][0, e].reshape(4, P, 2, 512).transpose(2, 1, 0, 3).reshape(2, P, UNIT)
    return out


def feature_major(a):
    return np.ascontiguousarray(a.reshape(T, -1, P).transpose(2, 1, 0))


def kernel(**inputs):
    import concourse.bacc as bacc
    from concourse.bass_utils import run_bass_kernel_spmd as run

    inp = {k: np.asarray(v) for k, v in inputs.items()}
    con, strict, levels, freq = constants()
    rows = lambda a: np.broadcast_to(np.asarray(a).reshape(1, -1), (P, np.asarray(a).size))
    lam = np.zeros((P, 16), np.float32)
    for k, n in enumerate(("diff_lam_q1_2", "diff_lam_k1_2", "diff_lam_q2_2", "diff_lam_k2_2")):
        lam[0:64, 4 * k:4 * k + 4] = inp[n][0].T
    vecs = [
        columns(inp["norm_g"]), columns(inp["ssm_conv_w"]), columns(inp["ssm_conv_b"]),
        columns(np.repeat(inp["ssm_D"][0], SSM_P)), columns(inp["ssm_norm_g"]), columns(inp["cf_pw1_b"]),
        columns(inp["cf_dw_w"]), columns(inp["cf_dw_b"]), columns(inp["cf_ln_g"]), columns(inp["cf_ln_b"]),
        columns(inp["cf_pw2_b"]), columns(inp["xa_mem_g"]), columns(inp["ffn_conv_w"]), columns(inp["ffn_conv_b"]),
        columns(inp["attn_norm_2"]), lam, columns(inp["diff_subln_2"]), columns(inp["mlp_norm_2"]),
        columns(inp["ple_norm_2"]), columns(inp["final_norm_2"]), columns(inp["attn_norm_w_3"]),
        columns(inp["hg_lower_bound_3"]), columns(inp["hg_out_norm_w_3"]), columns(inp["mla_q_norm_w_3"]),
        columns(inp["mla_kv_norm_w_3"]), columns(inp["ffn_norm_w_3"]), columns(inp["final_norm_w_3"]),
        rows(inp["ssm_dt_bias"]), rows(inp["ssm_A_log"]), freq,
    ]
    wdt = inp["ssm_in_w"][0][:, 5120:].reshape(8, P, 32).transpose(1, 0, 2)
    wr = np.concatenate([inp["router_group_w_3"][0], inp["router_expert_w_3"][0]], 1).reshape(8, P, 72).transpose(1, 0, 2)
    rb = np.concatenate([inp["router_group_b_3"][0], inp["router_expert_b_3"][0]])
    arrays = {
        "x": feature_major(inp["x"][0]), "mem": feature_major(inp["mem"][0]),
        "vec": np.concatenate(vecs, 1).astype(np.float32), "con": con, "strict": strict, "levels": levels,
        "wdt": wdt, "router": np.concatenate([wr.reshape(P, -1), rows(rb)], 1),
        "p": np.stack([feature_major(inp["p_2"][l, 0]) for l in range(2)]),
        "pos2": np.broadcast_to(inp["positions_2"].astype(np.int32), (P, T)),
        "pos3": np.broadcast_to(inp["positions_3"].astype(np.int32), (P, T)),
        "stream": stream(inp),
    }
    arrays = {k: np.ascontiguousarray(v) for k, v in arrays.items()}
    nc = bacc.Bacc("TRN2", target_bir_lowering=False, num_devices=1)
    io = {}
    for k, v in arrays.items():
        io[k] = nc.dram_tensor(f"in_{k}", v.shape, mybir.dt.from_np(v.dtype), kind="ExternalInput").ap()
    io["out"] = nc.dram_tensor("out_0", (P, DC, T), F32, kind="ExternalOutput").ap()
    program(nc, io)
    r = run(nc, [{f"in_{k}": v for k, v in arrays.items()}], core_ids=[0])
    y = r.results[0]["out_0"]
    return np.ascontiguousarray(y.transpose(2, 1, 0)).reshape(1, T, D)
```
